# Optimizing a Trainium2 kernel written in Bass

```python
import math
import jax, jax.numpy as jnp
from jax import lax
import numpy as np

D_MODEL = 2048
BATCH = 1
SEQ = 256
DEPTH = 1

DA_HEADS = 4
DA_HD = 64
DA_W = DA_HEADS * 2 * DA_HD
SW_HEADS = 8
SW_KV = 2
SW_HD = 64
WINDOW = 128
SW_QW = SW_HEADS * SW_HD
SW_KW = SW_KV * SW_HD
MB_HEADS = 8
MB_HD = 64
MB_W = MB_HEADS * MB_HD
MB_BLOCK = 256
MB_TOPK = 3
MB_CHUNK = 32
Q_BLOCK = 128
N_BUCKETS = 32
MAX_DIST = 128
N_ATT_HEADS = DA_HEADS + SW_HEADS + MB_HEADS
N_BRANCH = 3
IN_W = 3 * DA_W + SW_QW + 2 * SW_KW + 3 * MB_W + N_BRANCH * D_MODEL
D_FF = 5632
CONV_W = 3
EPS = 1e-6


def rmsnorm(x, g):
    xf = x.astype(jnp.float32)
    y = xf * lax.rsqrt(jnp.mean(xf * xf, axis=-1, keepdims=True) + EPS)
    return (y * g.astype(jnp.float32)).astype(x.dtype)

def rel_bucket(dist):
    n = jnp.maximum(dist, 0)
    max_exact = N_BUCKETS // 2
    nf = jnp.maximum(n, 1).astype(jnp.float32)
    large = max_exact + (jnp.log(nf / max_exact) / math.log(MAX_DIST / max_exact)
                         * (N_BUCKETS - max_exact)).astype(jnp.int32)
    large = jnp.minimum(large, N_BUCKETS - 1)
    return jnp.where(n < max_exact, n, large)

def diff_attention(q, k, v, lam, lam_init, subln_g, bias_t):
    B, S = q.shape[0], q.shape[1]
    nb = S // Q_BLOCK
    scale = DA_HD ** -0.5
    qb = jnp.moveaxis(q.reshape(B, nb, Q_BLOCK, DA_HEADS, 2, DA_HD), 1, 0)
    kpos = jnp.arange(S)

    def block(args):
        qi, i = args
        qpos = i * Q_BLOCK + jnp.arange(Q_BLOCK)
        dist = qpos[:, None] - kpos[None, :]
        bias = jnp.take(bias_t, rel_bucket(dist), axis=1)
        logits = jnp.einsum('bqhmd,bkhmd->bhmqk', qi, k).astype(jnp.float32) * scale + bias[None, :, None]
        logits = jnp.where(dist >= 0, logits, -jnp.inf)
        p = jax.nn.softmax(logits, axis=-1)
        attn = p[:, :, 0] - lam * p[:, :, 1]
        return jnp.einsum('bhqk,bkhe->bqhe', attn.astype(v.dtype), v)

    o = lax.map(block, (qb, jnp.arange(nb)))
    o = jnp.moveaxis(o, 0, 1).reshape(B, S, DA_HEADS, 2 * DA_HD)
    o = rmsnorm(o, subln_g) * (1.0 - lam_init)
    return o.reshape(B, S, DA_W)

def sliding_window_attention(q, k, v, sinks, bias_t):
    B, S = q.shape[0], q.shape[1]
    nb = S // Q_BLOCK
    G = SW_HEADS // SW_KV
    scale = SW_HD ** -0.5
    qb = q.reshape(B, nb, Q_BLOCK, SW_KV, G, SW_HD)
    kb = k.reshape(B, nb, Q_BLOCK, SW_KV, SW_HD)
    vb = v.reshape(B, nb, Q_BLOCK, SW_KV, SW_HD)
    shift = lambda t: jnp.concatenate([jnp.zeros_like(t[:, :1]), t[:, :-1]], axis=1)
    kc = jnp.concatenate([shift(kb), kb], axis=2)
    vc = jnp.concatenate([shift(vb), vb], axis=2)
    blk = jnp.arange(nb)[:, None] * Q_BLOCK
    qpos = blk + jnp.arange(Q_BLOCK)[None]
    kpos = blk - Q_BLOCK + jnp.arange(2 * Q_BLOCK)[None]
    dist = qpos[:, :, None] - kpos[:, None, :]
    valid = (dist >= 0) & (dist < WINDOW) & (kpos[:, None, :] >= 0)
    bias = jnp.take(bias_t, rel_bucket(dist), axis=1)
    bias = jnp.moveaxis(bias.reshape(SW_KV, G, nb, Q_BLOCK, 2 * Q_BLOCK), 2, 0)
    logits = jnp.einsum('bnqkgd,bnskd->bnkgqs', qb, kc).astype(jnp.float32) * scale + bias[None]
    logits = jnp.where(valid[None, :, None, None], logits, -jnp.inf)
    sink = jnp.broadcast_to(sinks.astype(jnp.float32).reshape(1, 1, SW_KV, G, 1, 1),
                            logits.shape[:-1] + (1,))
    p = jax.nn.softmax(jnp.concatenate([logits, sink], axis=-1), axis=-1)[..., :-1]
    o = jnp.einsum('bnkgqs,bnskd->bnqkgd', p.astype(vc.dtype), vc)
    return o.reshape(B, S, SW_QW)

def moba_attention(q, k, v, bias_t):
    B, S = q.shape[0], q.shape[1]
    nblk = -(-S // MB_BLOCK)
    Sp = nblk * MB_BLOCK
    padw = ((0, 0), (0, Sp - S), (0, 0), (0, 0))
    q, k, v = [jnp.pad(t, padw).transpose(0, 2, 1, 3) for t in (q, k, v)]
    scale = MB_HD ** -0.5
    kblk = k.reshape(B, MB_HEADS, nblk, MB_BLOCK, MB_HD)
    vblk = v.reshape(B, MB_HEADS, nblk, MB_BLOCK, MB_HD)
    kmean = jnp.mean(kblk.astype(jnp.float32), axis=3)
    own = jnp.arange(Sp) // MB_BLOCK
    gate = jnp.einsum('bhtd,bhnd->bhtn', q.astype(jnp.float32), kmean)
    past = jnp.arange(nblk)[None, :] < own[:, None]
    gate = jnp.where(past, gate, -jnp.inf)
    topk = min(MB_TOPK, nblk)
    _, idx = lax.top_k(gate, topk)

    nch = Sp // MB_CHUNK
    per_blk = MB_BLOCK // MB_CHUNK
    qc = q.reshape(B, MB_HEADS, nch, MB_CHUNK, MB_HD).transpose(2, 0, 1, 3, 4)
    idxc = idx.reshape(B, MB_HEADS, nch, MB_CHUNK, topk).transpose(2, 0, 1, 3, 4)
    bi = jnp.arange(B)[:, None, None, None]
    hi = jnp.arange(MB_HEADS)[None, :, None, None]
    hi5 = hi[..., None]
    s_off = jnp.arange(MB_BLOCK)

    def chunk(args):
        qi, ii, c = args
        qpos = c * MB_CHUNK + jnp.arange(MB_CHUNK)
        ob = c // per_blk
        ks = kblk[bi, hi, ii]
        vs = vblk[bi, hi, ii]
        dist_s = qpos[None, None, :, None, None] - (ii[..., None] * MB_BLOCK + s_off)
        ls = (jnp.einsum('bhcd,bhcjsd->bhcjs', qi, ks).astype(jnp.float32) * scale
              + bias_t[hi5, rel_bucket(dist_s)])
        ls = jnp.where((jnp.arange(topk) < ob)[:, None], ls, -jnp.inf)
        ls = ls.reshape(B, MB_HEADS, MB_CHUNK, topk * MB_BLOCK)
        ko = lax.dynamic_slice_in_dim(k, ob * MB_BLOCK, MB_BLOCK, axis=2)
        vo = lax.dynamic_slice_in_dim(v, ob * MB_BLOCK, MB_BLOCK, axis=2)
        dist_o = qpos[:, None] - (ob * MB_BLOCK + s_off)[None, :]
        lo = (jnp.einsum('bhcd,bhsd->bhcs', qi, ko).astype(jnp.float32) * scale
              + jnp.take(bias_t, rel_bucket(dist_o), axis=1)[None])
        lo = jnp.where(dist_o >= 0, lo, -jnp.inf)
        p = jax.nn.softmax(jnp.concatenate([ls, lo], axis=-1), axis=-1).astype(vs.dtype)
        ps = p[..., :topk * MB_BLOCK].reshape(B, MB_HEADS, MB_CHUNK, topk, MB_BLOCK)
        po = p[..., topk * MB_BLOCK:]
        return (jnp.einsum('bhcjs,bhcjsd->bhcd', ps, vs)
                + jnp.einsum('bhcs,bhsd->bhcd', po, vo))

    o = lax.map(chunk, (qc, idxc, jnp.arange(nch)))
    o = o.transpose(1, 0, 3, 2, 4).reshape(B, Sp, MB_W)
    return o[:, :S]

def conv_ffn(h, w_up, conv_w, conv_b, w_down):
    S = h.shape[1]
    u = h @ w_up
    up = jnp.pad(u, ((0, 0), (CONV_W - 1, 0), (0, 0)))
    c = conv_b
    for i in range(CONV_W):
        c = c + up[:, i:i + S] * conv_w[i]
    gate, val = jnp.split(c, 2, axis=-1)
    return (jax.nn.gelu(gate, approximate=True) * val) @ w_down

def first_inputs(seed: int = 0) -> dict:
    key = jax.random.key(seed)
    ks = jax.random.split(key, 24)
    f32 = jnp.float32
    nrm = lambda k, shape, s: jax.random.normal(k, shape, f32) * s
    gain = lambda k: 1.0 + nrm(k, (DEPTH, D_MODEL), 0.02)
    return {
        "x": nrm(ks[0], (BATCH, SEQ, D_MODEL), 1.0),
        "rel_bias_table": nrm(ks[1], (N_BUCKETS, N_ATT_HEADS), 0.5),
        "w_in": nrm(ks[2], (DEPTH, D_MODEL, IN_W), D_MODEL ** -0.5),
        "b_gate": nrm(ks[3], (DEPTH, N_BRANCH * D_MODEL), 0.1),
        "lam_q1": nrm(ks[4], (DEPTH, DA_HD), 0.1),
        "lam_k1": nrm(ks[5], (DEPTH, DA_HD), 0.1),
        "lam_q2": nrm(ks[6], (DEPTH, DA_HD), 0.1),
        "lam_k2": nrm(ks[7], (DEPTH, DA_HD), 0.1),
        "diff_subln_g": 1.0 + nrm(ks[8], (DEPTH, 2 * DA_HD), 0.02),
        "sinks": nrm(ks[9], (DEPTH, SW_HEADS), 0.5),
        "w_oa": nrm(ks[10], (DEPTH, DA_W, D_MODEL), DA_W ** -0.5),
        "w_ob": nrm(ks[11], (DEPTH, SW_QW, D_MODEL), SW_QW ** -0.5),
        "w_oc": nrm(ks[12], (DEPTH, MB_W, D_MODEL), MB_W ** -0.5),
        "w_out": nrm(ks[13], (DEPTH, D_MODEL, D_MODEL), D_MODEL ** -0.5),
        "pre_mix_g": gain(ks[14]),
        "post_mix_g": gain(ks[15]),
        "pre_ffn_g": gain(ks[16]),
        "post_ffn_g": gain(ks[17]),
        "w_up": nrm(ks[18], (DEPTH, D_MODEL, 2 * D_FF), D_MODEL ** -0.5),
        "conv_w": nrm(ks[19], (DEPTH, CONV_W, 2 * D_FF), CONV_W ** -0.5),
        "conv_b": nrm(ks[20], (DEPTH, 2 * D_FF), 0.02),
        "w_down": nrm(ks[21], (DEPTH, D_FF, D_MODEL), D_FF ** -0.5),
    }

def first_block(x, rel_bias_table, w_in, b_gate, lam_q1, lam_k1, lam_q2, lam_k2, diff_subln_g,
              sinks, w_oa, w_ob, w_oc, w_out, pre_mix_g, post_mix_g, pre_ffn_g, post_ffn_g,
              w_up, conv_w, conv_b, w_down):
    B, S = x.shape[0], x.shape[1]
    tab_t = rel_bias_table.T
    tab_a = tab_t[:DA_HEADS]
    tab_b = tab_t[DA_HEADS:DA_HEADS + SW_HEADS]
    tab_c = tab_t[DA_HEADS + SW_HEADS:]
    cuts = list(np.cumsum([DA_W, DA_W, DA_W, SW_QW, SW_KW, SW_KW, MB_W, MB_W, MB_W]))
    for l in range(DEPTH):
        h = rmsnorm(x, pre_mix_g[l])
        proj = h @ w_in[l]
        qa, ka, va, qb, kb, vb, qc, kc, vc, g = jnp.split(proj, cuts, axis=-1)
        gates = jax.nn.sigmoid((g + b_gate[l]).astype(jnp.float32)).astype(x.dtype)
        ga, gb, gc = jnp.split(gates, N_BRANCH, axis=-1)

        lam_init = 0.8 - 0.6 * math.exp(-0.3 * l)
        lam = (jnp.exp(jnp.sum(lam_q1[l].astype(jnp.float32) * lam_k1[l].astype(jnp.float32)))
               - jnp.exp(jnp.sum(lam_q2[l].astype(jnp.float32) * lam_k2[l].astype(jnp.float32)))
               + lam_init)
        ya = diff_attention(qa.reshape(B, S, DA_HEADS, 2, DA_HD), ka.reshape(B, S, DA_HEADS, 2, DA_HD),
                            va.reshape(B, S, DA_HEADS, 2 * DA_HD), lam, lam_init, diff_subln_g[l], tab_a)
        yb = sliding_window_attention(qb.reshape(B, S, SW_HEADS, SW_HD), kb.reshape(B, S, SW_KV, SW_HD),
                                      vb.reshape(B, S, SW_KV, SW_HD), sinks[l], tab_b)
        yc = moba_attention(qc.reshape(B, S, MB_HEADS, MB_HD), kc.reshape(B, S, MB_HEADS, MB_HD),
                            vc.reshape(B, S, MB_HEADS, MB_HD), tab_c)
        mix = ga * (ya @ w_oa[l]) + gb * (yb @ w_ob[l]) + gc * (yc @ w_oc[l])
        x = x + rmsnorm(mix @ w_out[l], post_mix_g[l])
        h = rmsnorm(x, pre_ffn_g[l])
        x = x + rmsnorm(conv_ffn(h, w_up[l], conv_w[l], conv_b[l], w_down[l]), post_ffn_g[l])
    return x


DEPTH_2 = 2

SB_HEADS = 8
SB_HEAD_DIM = 128
SB_WIDTH = SB_HEADS * SB_HEAD_DIM
POOL_WINDOWS = (2, 4, 8, 16)
POOL_GROUPS = len(POOL_WINDOWS)
POOL_WIDTH = D_MODEL - SB_WIDTH
POOL_GROUP_DIM = POOL_WIDTH // POOL_GROUPS
MIX_WIDTH = SB_WIDTH + POOL_WIDTH
EVEN_IN = 4 * SB_WIDTH + 2 * POOL_WIDTH
BLOCK_Q = 128

RWKV_HEAD_DIM = 64
RWKV_HEADS = D_MODEL // RWKV_HEAD_DIM
DECAY_LORA = 96
ICLR_LORA = 96
GN_EPS = 64e-5
L2_EPS = 1e-12

LN_EPS = 1e-5
DEEPNORM_ALPHA = (2 * DEPTH_2) ** 0.25
DEEPNORM_BETA = (8 * DEPTH_2) ** -0.25
N_EVEN = (DEPTH_2 + 1) // 2
N_ODD = DEPTH_2 // 2


def layer_norm(x, g, b):
    xf = x.astype(jnp.float32)
    mean = jnp.mean(xf, axis=-1, keepdims=True)
    var = jnp.mean(jnp.square(xf - mean), axis=-1, keepdims=True)
    return ((xf - mean) * lax.rsqrt(var + LN_EPS) * g + b).astype(x.dtype)

def stick_breaking_attention(q, k, v):
    S = q.shape[2]
    scale = SB_HEAD_DIM ** -0.5
    outs = []
    for start in range(0, S, BLOCK_Q):
        end = start + BLOCK_Q
        qb = q[:, :, start:end].astype(jnp.float32)
        kb = k[:, :, :end].astype(jnp.float32)
        vb = v[:, :, :end]
        z = jnp.einsum('bhqd,bhkd->bhqk', qb, kb) * scale
        t_idx = start + jnp.arange(BLOCK_Q)[:, None]
        s_idx = jnp.arange(end)[None, :]
        causal = s_idx < t_idx
        log_keep = jnp.where(causal, jax.nn.log_sigmoid(-z), 0.0)
        later = lax.cumsum(log_keep, axis=3, reverse=True) - log_keep
        weights = jnp.where(causal, jnp.exp(jax.nn.log_sigmoid(z) + later), 0.0)
        outs.append(jnp.einsum('bhqk,bhkd->bhqd', weights.astype(vb.dtype), vb))
    return jnp.concatenate(outs, axis=2)

def multiscale_pool(u, w_pool, pool_scale):
    B_, S, _ = u.shape
    ug = u.reshape(B_, S, POOL_GROUPS, POOL_GROUP_DIM).astype(jnp.float32)
    c0 = jnp.concatenate([jnp.zeros_like(ug[:, :1]), jnp.cumsum(ug, axis=1)], axis=1)
    pos = jnp.arange(1, S + 1, dtype=jnp.float32)
    outs = []
    for g, w in enumerate(POOL_WINDOWS):
        cg = c0[:, :, g]
        lower = jnp.concatenate([jnp.zeros_like(cg[:, :w - 1]), cg[:, :S - w + 1]], axis=1)
        count = jnp.minimum(pos, float(w))[None, :, None]
        outs.append((cg[:, 1:] - lower) / count - ug[:, :, g])
    pooled = jnp.stack(outs, axis=2)
    mixed = jnp.einsum('bsgc,gcd->bsgd', pooled, w_pool.astype(jnp.float32))
    return (mixed.reshape(B_, S, POOL_WIDTH) * pool_scale).astype(u.dtype)

def even_layer(x, w_in, w_pool, pool_scale, w_out):
    B_, S, _ = x.shape
    h = x @ w_in
    q, k, v, g_a, u, g_b = jnp.split(
        h, [SB_WIDTH, 2 * SB_WIDTH, 3 * SB_WIDTH, 4 * SB_WIDTH, 4 * SB_WIDTH + POOL_WIDTH], axis=-1)

    def heads(t):
        return t.reshape(B_, S, SB_HEADS, SB_HEAD_DIM).transpose(0, 2, 1, 3)

    o_a = stick_breaking_attention(heads(q), heads(k), heads(v))
    o_a = o_a.transpose(0, 2, 1, 3).reshape(B_, S, SB_WIDTH)
    o_b = multiscale_pool(u, w_pool, pool_scale)
    mixed = jnp.concatenate([o_a * jax.nn.silu(g_a), o_b * jax.nn.silu(g_b)], axis=-1)
    return mixed @ w_out

def wkv7_scan(r, w, k, v, kk, a):
    B_, S, H, N = r.shape

    def step(state, inp):
        r_t, w_t, k_t, v_t, kk_t, a_t = inp
        sa = jnp.einsum('bhvk,bhk->bhv', state, -kk_t)
        state = (state * w_t[:, :, None, :]
                 + sa[..., None] * (kk_t * a_t)[:, :, None, :]
                 + v_t[..., None] * k_t[:, :, None, :])
        return state, jnp.einsum('bhvk,bhk->bhv', state, r_t)

    xs = (jnp.moveaxis(r, 1, 0), jnp.moveaxis(w, 1, 0), jnp.moveaxis(k, 1, 0),
          jnp.moveaxis(v, 1, 0), jnp.moveaxis(kk, 1, 0), jnp.moveaxis(a, 1, 0))
    state0 = jnp.zeros((B_, H, N, N), jnp.float32)
    _, out = lax.scan(step, state0, xs)
    return jnp.moveaxis(out, 0, 1)

def odd_layer(x, mu, w_r, w_k, w_v, w_g, w0, w1, w2, a0, a1, a2, k_k, k_a, r_k, gn_w, gn_b, w_o):
    B_, S, D = x.shape
    H, N = RWKV_HEADS, RWKV_HEAD_DIM
    f32 = jnp.float32
    x_prev = jnp.pad(x, ((0, 0), (1, 0), (0, 0)))[:, :S]
    xx = x_prev - x
    xr = x + xx * mu[0]
    xw = x + xx * mu[1]
    xk = x + xx * mu[2]
    xv = x + xx * mu[3]
    xa = x + xx * mu[4]
    xg = x + xx * mu[5]
    r = (xr @ w_r).astype(f32)
    k = (xk @ w_k).astype(f32)
    v = (xv @ w_v).astype(f32)
    g = (xg @ w_g).astype(f32)
    w_log = -jax.nn.softplus(-(w0 + jnp.tanh(xw @ w1) @ w2).astype(f32)) - 0.5
    decay = jnp.exp(-jnp.exp(w_log))
    a = jax.nn.sigmoid((a0 + (xa @ a1) @ a2).astype(f32))
    kk = (k * k_k).reshape(B_, S, H, N)
    kk = kk / jnp.maximum(jnp.sqrt(jnp.sum(kk * kk, axis=-1, keepdims=True)), L2_EPS)
    k = k * (1.0 + (a - 1.0) * k_a)
    r = r.reshape(B_, S, H, N)
    k = k.reshape(B_, S, H, N)
    v = v.reshape(B_, S, H, N)
    o = wkv7_scan(r, decay.reshape(B_, S, H, N), k, v, kk, a.reshape(B_, S, H, N))
    mean = jnp.mean(o, axis=-1, keepdims=True)
    var = jnp.mean(jnp.square(o - mean), axis=-1, keepdims=True)
    o = ((o - mean) * lax.rsqrt(var + GN_EPS)).reshape(B_, S, D) * gn_w + gn_b
    bonus = jnp.sum(r * k * r_k, axis=-1, keepdims=True) * v
    o = (o + bonus.reshape(B_, S, D)) * jax.nn.silu(g)
    return o.astype(x.dtype) @ w_o

def second_inputs(seed: int = 0) -> dict:
    key = jax.random.key(seed)
    ks = list(jax.random.split(key, 32))
    f32 = jnp.float32

    def nrm(i, shape, scale):
        return scale * jax.random.normal(ks[i], shape, f32)

    def unif(i, shape, lo, hi):
        return jax.random.uniform(ks[i], shape, f32, lo, hi)

    D = D_MODEL
    H, N = RWKV_HEADS, RWKV_HEAD_DIM
    return {
        'x': nrm(0, (BATCH, SEQ, D), 1.0),
        'ev_w_in': nrm(1, (N_EVEN, D, EVEN_IN), D ** -0.5),
        'ev_w_pool': nrm(2, (N_EVEN, POOL_GROUPS, POOL_GROUP_DIM, POOL_GROUP_DIM), POOL_GROUP_DIM ** -0.5),
        'ev_pool_scale': 1.0 + nrm(3, (N_EVEN, POOL_WIDTH), 0.1),
        'ev_w_out': nrm(4, (N_EVEN, MIX_WIDTH, D), DEEPNORM_BETA * MIX_WIDTH ** -0.5),
        'od_mu': unif(5, (N_ODD, 6, D), 0.0, 1.0),
        'od_w_r': nrm(6, (N_ODD, D, D), D ** -0.5),
        'od_w_k': nrm(7, (N_ODD, D, D), D ** -0.5),
        'od_w_v': nrm(8, (N_ODD, D, D), D ** -0.5),
        'od_w_g': nrm(9, (N_ODD, D, D), D ** -0.5),
        'od_w0': unif(10, (N_ODD, D), -6.0, 1.0),
        'od_w1': nrm(11, (N_ODD, D, DECAY_LORA), D ** -0.5),
        'od_w2': nrm(12, (N_ODD, DECAY_LORA, D), 0.5 * DECAY_LORA ** -0.5),
        'od_a0': nrm(13, (N_ODD, D), 0.1),
        'od_a1': nrm(14, (N_ODD, D, ICLR_LORA), D ** -0.5),
        'od_a2': nrm(15, (N_ODD, ICLR_LORA, D), 0.5 * ICLR_LORA ** -0.5),
        'od_k_k': 0.85 + nrm(16, (N_ODD, D), 0.05),
        'od_k_a': 1.0 + nrm(17, (N_ODD, D), 0.05),
        'od_r_k': nrm(18, (N_ODD, H, N), 0.1),
        'od_gn_w': 1.0 + nrm(19, (N_ODD, D), 0.05),
        'od_gn_b': nrm(20, (N_ODD, D), 0.02),
        'od_w_o': nrm(21, (N_ODD, D, D), DEEPNORM_BETA * D ** -0.5),
        'ln_g': 1.0 + nrm(22, (DEPTH_2, D), 0.02),
        'ln_b': nrm(23, (DEPTH_2, D), 0.02),
    }

def second_block(x, ev_w_in, ev_w_pool, ev_pool_scale, ev_w_out,
              od_mu, od_w_r, od_w_k, od_w_v, od_w_g, od_w0, od_w1, od_w2,
              od_a0, od_a1, od_a2, od_k_k, od_k_a, od_r_k, od_gn_w, od_gn_b, od_w_o,
              ln_g, ln_b):
    for layer in range(DEPTH_2):
        j = layer // 2
        if layer % 2 == 0:
            y = even_layer(x, ev_w_in[j], ev_w_pool[j], ev_pool_scale[j], ev_w_out[j])
        else:
            y = odd_layer(x, od_mu[j], od_w_r[j], od_w_k[j], od_w_v[j], od_w_g[j],
                          od_w0[j], od_w1[j], od_w2[j], od_a0[j], od_a1[j], od_a2[j],
                          od_k_k[j], od_k_a[j], od_r_k[j], od_gn_w[j], od_gn_b[j], od_w_o[j])
        x = layer_norm(DEEPNORM_ALPHA * x + y, ln_g[layer], ln_b[layer])
    return x


def setup_inputs(seed=0):
    out = dict(first_inputs(seed))
    for name, value in second_inputs(seed + 1).items():
        if name != "x":
            out[name + "_2"] = value
    return out


def reference(
    x, rel_bias_table, w_in, b_gate, lam_q1, lam_k1, lam_q2, lam_k2, diff_subln_g, sinks, w_oa,
    w_ob, w_oc, w_out, pre_mix_g, post_mix_g, pre_ffn_g, post_ffn_g, w_up, conv_w, conv_b,
    w_down, ev_w_in_2, ev_w_pool_2, ev_pool_scale_2, ev_w_out_2, od_mu_2, od_w_r_2, od_w_k_2,
    od_w_v_2, od_w_g_2, od_w0_2, od_w1_2, od_w2_2, od_a0_2, od_a1_2, od_a2_2, od_k_k_2,
    od_k_a_2, od_r_k_2, od_gn_w_2, od_gn_b_2, od_w_o_2, ln_g_2, ln_b_2,
):
    x = first_block(
        x, rel_bias_table, w_in, b_gate, lam_q1, lam_k1, lam_q2, lam_k2, diff_subln_g, sinks,
        w_oa, w_ob, w_oc, w_out, pre_mix_g, post_mix_g, pre_ffn_g, post_ffn_g, w_up, conv_w,
        conv_b, w_down,
    )
    return second_block(
        x, ev_w_in_2, ev_w_pool_2, ev_pool_scale_2, ev_w_out_2, od_mu_2, od_w_r_2, od_w_k_2,
        od_w_v_2, od_w_g_2, od_w0_2, od_w1_2, od_w2_2, od_a0_2, od_a1_2, od_a2_2, od_k_k_2,
        od_k_a_2, od_r_k_2, od_gn_w_2, od_gn_b_2, od_w_o_2, ln_g_2, ln_b_2,
    )


_drawn_inputs = setup_inputs


def setup_inputs(seed=0):
    import zlib

    import numpy as np

    out = dict(_drawn_inputs(seed))
    spreads = {}
    factors = {'diff_subln_g': 3.129,
     'sinks': 5.254,
     'post_mix_g': 2.949,
     'pre_ffn_g': 3.091,
     'post_ffn_g': 4.315,
     'conv_b': 2.994,
     'od_w1_2': 8.0,
     'od_w2_2': 8.0,
     'od_a0_2': 7.562,
     'od_k_k_2': 23.03,
     'od_k_a_2': 4.981,
     'od_gn_w_2': 6.75,
     'od_gn_b_2': 25.304}
    for name, (base, spread) in spreads.items():
        noise = np.random.default_rng([zlib.crc32(name.encode()), seed]).standard_normal(out[name].shape)
        drawn = base * np.exp(spread * noise) if base else spread * noise
        out[name] = __import__('jax').numpy.asarray(drawn.astype(out[name].dtype))
    for name, factor in factors.items():
        out[name] = (out[name] * factor).astype(out[name].dtype)
    return out
```

```python
import math
from contextlib import ExitStack

import numpy as np

import concourse.bass as bass
from concourse import mybir

F32 = mybir.dt.float32
F32R = mybir.dt.float32r
ALU = mybir.AluOpType
ACT = mybir.ActivationFunctionType
AX = mybir.AxisListType

D = 2048
KT = D // 128
S = 256
D_FF = 5632
FT_TILES = D_FF // 128
PANEL = 512
EPS = 1e-6
LN_EPS = 1e-5
GN_EPS = 64e-5
NEG = -1e30
N_BUCKETS = 32
MAX_DIST = 128
N_HEADS_1 = 20
ALPHA = 4 ** 0.25
POOL_WINDOWS = (2, 4, 8, 16)
LORA = 96


def bucket_rows():
    i = np.arange(384)
    dist = 255 - i
    n = np.maximum(dist, 0)
    half = N_BUCKETS // 2
    nf = np.maximum(n, 1).astype(np.float32)
    large = half + (np.log(nf / np.float32(half)) / np.float32(math.log(MAX_DIST / half))
                    * np.float32(N_BUCKETS - half)).astype(np.int32)
    bucket = np.where(n < half, n, np.minimum(large, N_BUCKETS - 1))
    rows = np.zeros((128, 384), np.float32)
    rows[bucket, i] = 1.0
    rows[:32, dist < 0] = 0.0
    rows[32] = dist < 0
    rows[33] = dist >= 128
    return rows


def constant_tables():
    r = np.arange(128)
    eye = np.eye(128, dtype=np.float32)
    flip = eye[::-1].copy()
    marks = np.zeros((128, 20), np.float32)
    marks[32] = NEG
    marks[33, 4:12] = NEG
    t = {"ident": eye, "flip": flip, "buckets": bucket_rows(), "marks": marks}
    t["suffix"] = -(r[:, None] >= r[None, :]).astype(np.float32)
    t["minus_ones"] = -np.ones((128, 128), np.float32)
    for g, w in enumerate(POOL_WINDOWS):
        tp, tq = np.arange(256)[:, None], np.arange(256)[None, :]
        m = ((tp <= tq) & (tp > tq - w)) / np.minimum(tq + 1, w).astype(np.float32)
        m = (m - (tp == tq)).astype(np.float32)
        t[f"pool{g}a"] = m[:128]
        t[f"pool{g}b"] = m[128:, 128:]
    t["hidden"] = (NEG * (r[:, None] >= r[None, :])).astype(np.float32)
    for k in range(7):
        a, b = r[:, None] >> k, r[None, :] >> k
        t[f"level{k}"] = ((a == b + 1) & (b % 2 == 0)).astype(np.float32)
    t["level0t"] = t["level0"].T.copy()
    t["before"] = (r[:, None] < r[None, :]).astype(np.float32)
    t["upto"] = (r[:, None] <= r[None, :]).astype(np.float32)
    t["centred"] = t["upto"] - (r[:, None] < 64).astype(np.float32)
    sel = np.zeros((128, 2), np.float32)
    sel[64:, 0] = 1.0
    sel[:64, 1] = 1.0
    t["halves"] = sel
    return t


def table_layout():
    at, out = 0, {}
    for name, a in constant_tables().items():
        out[name] = (at, a.shape[1])
        at += a.shape[1]
    return out, at


class Job:

    def __init__(self, name, weights, panels, chunks, stationary, looped):
        self.name, self.panels, self.chunks = name, panels, chunks
        self.weights = weights
        self.stationary = stationary
        self.looped = looped
        self.g0 = self.p0 = 0

    def place(self, g0, p0):
        self.g0, self.p0 = g0, p0
        return g0 + self.panels * self.chunks, p0 + self.panels


def build(nc, a, segments="ABCD"):
    ctx = ExitStack()
    tables, table_cols = table_layout()
    KB = 1024
    BASE = 16512
    PH = 87

    def at(name, shape, dt, kb):
        return nc.alloc_sbuf_tensor_at(name, shape, dt, offset=BASE + int(kb * KB))

    semaphores = {}

    def sem(name):
        if name not in semaphores:
            semaphores[name] = ctx.enter_context(nc.semaphore(name))
        return semaphores[name]

    def dram(name, shape):
        return nc.dram_tensor(name, shape, F32, kind="Internal").ap()

    def table(name):
        c, w = tables[name]
        return a["tables"][:, c:c + w]

    raw = [at(f"raw{i}", [128, 4, PANEL], F32, 8 * i) for i in range(4)]
    wh = [at(f"w_high{i}", [128, 4, PANEL], F32R, 32 + 8 * i) for i in range(2)]
    wl = [at(f"w_low{i}", [128, 4, PANEL], F32R, 48 + 8 * i) for i in range(2)]
    X = at("X", [128, 2, D], F32, 64)
    ident = at("ident", [128, 128], F32, 80)
    gains = at("gains", [128, 128], F32, 80.5)
    conv = at("conv", [128, 4, 88], F32, 81)
    stat = at("stat", [128, 128], F32, 82.5)
    nstat = at("nstat", [128, 96], F32, 83)
    small = at("small", [128, 128], F32, 83.5)
    vec_in = at("vec_in", [128, 128], F32, 84)
    conv_in = at("conv_in", [88, 4, 128], F32, 84.5)

    PS = [ctx.enter_context(nc.psum_tensor(f"bank{i}", [128, 512], F32)) for i in range(8)]

    jobs = []
    plan = {}

    def add_job(name, weights, panels, chunks, stationary, looped):
        j = Job(name, weights, panels, chunks, stationary, looped)
        g, p = (jobs[-1].g0 + jobs[-1].panels * jobs[-1].chunks,
                jobs[-1].p0 + jobs[-1].panels) if jobs else (0, 0)
        j.place(g, p)
        jobs.append(j)
        plan[name] = j

    def kview(w):
        return w.rearrange("(k p) n -> p k n", p=128)

    def chunk_of(g):
        for j in jobs:
            if g < j.g0 + j.panels * j.chunks:
                return j, (g - j.g0) // j.chunks, (g - j.g0) % j.chunks
        return None, 0, 0

    def width_of(g):
        j, p, _ = chunk_of(g)
        return 0 if j is None else j.weights(p)[3]

    def load_weights(sp):
        for j in jobs:
            def one(p, g, c, wait=True, slot=0):
                w, k0, col, width = j.weights(p)
                if wait:
                    sp.wait_ge(sem("w_low_made"), g - 3)
                sp.dma_start(raw[slot][:, :, 0:width],
                             w[:, k0 + 4 * c:k0 + 4 * c + 4, bass.ds(col, width)]
                             ).then_inc(sem(f"raw_loaded{slot}"), 16)

            if not j.looped:
                for p in range(j.panels):
                    for c in range(j.chunks):
                        if j.name == "odd_out" and p == 0 and c == 2:
                            group_loads(sp)
                            await_step(sp, "post_pool", "out", GROUPS - 1)
                        g = j.g0 + p * j.chunks + c
                        one(p, g, c, g >= 4, g % 4)
            else:
                first = 0
                if j.g0 == 0:
                    for p in range(j.looped):
                        for c in range(j.chunks):
                            g = p * j.chunks + c
                            one((0, p), g, c, g >= 4, g % 4)
                    first = 1
                with sp.Fori(first, j.panels // j.looped) as i:
                    for q in range(j.looped):
                        for c in range(j.chunks):
                            n = q * j.chunks + c
                            one(i * j.looped + q if j.looped == 1 else (i, q),
                                i * (j.looped * j.chunks) + (j.g0 + n), c, True, n % 4)

    def split_high(act, g, slot, width, first_uses):
        act.wait_ge(sem(f"raw_loaded{slot}"), first_uses)
        act.wait_ge(sem("w_used"), g - 1) if not (isinstance(g, int) and g < 2) else None
        act.activation(wh[slot % 2][:, :, 0:width], raw[slot][:, :, 0:width], ACT.Copy
                       ).then_inc(sem("w_high_made"), 1)

    def split_low(vec, g, slot, width):
        vec.wait_ge(sem("w_high_made"), g + 1)
        vec.tensor_tensor(wl[slot % 2][:, :, 0:width], raw[slot][:, :, 0:width],
                          wh[slot % 2][:, :, 0:width].bitcast(F32), ALU.subtract
                          ).then_inc(sem("w_low_made"), 1)

    def splits(eng, high, j, g_rel, count, i=None):
        for n in range(g_rel + 2, g_rel + 2 + count):
            g_static = j.g0 + n
            slot = g_static % 4
            if i is None:
                w = width_of(g_static)
                if not w:
                    continue
                if high:
                    split_high(eng, g_static, slot, w, 16 * (g_static // 4 + 1))
                else:
                    split_low(eng, g_static, slot, w)
            else:
                per = j.looped * j.chunks
                last = j.g0 + (j.panels // j.looped - 1) * per + n
                w = PANEL
                if not width_of(last):
                    raise ValueError("a looped job cannot end the stream")
                if high:
                    split_high(eng, i * per + g_static, slot, w, i * (4 * per) + 16 * (g_static // 4 + 1))
                else:
                    split_low(eng, i * per + g_static, slot, w)

    def splits_begin(eng, high):
        for g in range(2):
            slot = g % 4
            if high:
                split_high(eng, g, slot, width_of(g), 16)
            else:
                split_low(eng, g, slot, width_of(g))

    def panel_products(pe, j, p_static, g, P, ready=None):
        width = j.weights(p_static)[3]
        par = (j.p0 + (p_static if isinstance(p_static, int) else p_static[1])) % 2
        acc = [PS[2 * par + t] for t in range(2)]
        pe.wait_ge(sem("acc_free"), P + 1)
        for c in range(j.chunks):
            slot = (j.g0 + (p_static if isinstance(p_static, int) else p_static[1]) * j.chunks + c) % 4 % 2
            hi, lo, k0 = j.stationary(p_static, c)
            pe.wait_ge(sem("w_low_made"), g + (c + 1))
            for k in range(4):
                if ready is not None:
                    ready(c, k)
                for t in range(2):
                    xh = hi[:, k0 + k, 128 * t:128 * t + 128]
                    xl = lo[:, k0 + k, 128 * t:128 * t + 128]
                    b = acc[t][:, 0:width]
                    pe.matmul(b, xh, wh[slot][:, k, 0:width], start=(c == 0 and k == 0), stop=False)
                    pe.matmul(b, xh, wl[slot][:, k, 0:width], start=False, stop=False)
                    mm = pe.matmul(b, xl, wh[slot][:, k, 0:width], start=False,
                                   stop=(c == j.chunks - 1 and k == 3))
            mm.then_inc(sem("w_used"), 1)

    def evacuate(act, j, p_static, g_end, out, free=None):
        width = j.weights(p_static)[3]
        par = (j.p0 + (p_static if isinstance(p_static, int) else p_static[1])) % 2
        if free is not None:
            free()
        act.wait_ge(sem("w_used"), g_end)
        act.activation(out(0), PS[2 * par][:, 0:width], ACT.Copy)
        act.activation(out(1), PS[2 * par + 1][:, 0:width], ACT.Copy).then_inc(sem("acc_free"), 1)

    def run_pe(pe, j, ready_first=None, between=None):
        if not j.looped:
            for p in range(j.panels):
                r = ready_first if p == 0 else None
                panel_products(pe, j, p, j.g0 + p * j.chunks, j.p0 + p, r)
                if between:
                    between(p)
            return
        if ready_first is not None:
            ready_first(None, None)
        with pe.Fori(0, j.panels // j.looped) as i:
            for q in range(j.looped):
                panel_products(pe, j, (i, q), i * (j.looped * j.chunks) + (j.g0 + q * j.chunks),
                               i * j.looped + (j.p0 + q))

    def run_act(act, j, out, free=None, post=None, each=None):
        if not j.looped:
            for p in range(j.panels):
                for c in range(p * j.chunks, (p + 1) * j.chunks):
                    splits(act, True, j, c, 1)
                    if each:
                        each(c)
                evacuate(act, j, p, j.g0 + (p + 1) * j.chunks, lambda t: out(p, t),
                         None if free is None else lambda: free(p))
                if post:
                    post(p)
            return
        per = j.looped * j.chunks
        with act.Fori(0, j.panels // j.looped) as i:
            for q in range(j.looped):
                splits(act, True, j, q * j.chunks, j.chunks, i)
                evacuate(act, j, (i, q), i * per + (j.g0 + (q + 1) * j.chunks),
                         lambda t: out((i, q), t), None if free is None else lambda: free((i, q)))
                if post:
                    post((i, q))

    def run_vec(vec, j, post=None, each=None):
        if not j.looped:
            for p in range(j.panels):
                for c in range(p * j.chunks, (p + 1) * j.chunks):
                    splits(vec, False, j, c, 1)
                    if each:
                        each(c)
                if post:
                    post(p)
            return
        with vec.Fori(0, j.panels // j.looped) as i:
            for q in range(j.looped):
                splits(vec, False, j, q * j.chunks, j.chunks, i)
                if post:
                    post((i, q))

    def panel_number(j, p):
        return j.p0 + p if isinstance(p, int) else p[0] * j.looped + (j.p0 + p[1])

    def panel_index(j, p):
        return p if isinstance(p, int) else p[0] * j.looped + p[1]

    class Turn:

        count = high = 0

        def __init__(self, tiles, split):
            self.tiles, self.split = tiles, split
            self.first, self.first_high = Turn.count, Turn.high
            Turn.count += tiles // 2
            Turn.high += tiles // 2 if split else 0

    Turn.count = Turn.high = 0

    def turn_pe(pe, turn, src, ready):
        for n in range(turn.tiles // 2):
            m = turn.first + n
            ready(n)
            if m >= 4:
                pe.wait_ge(sem("turned_read"), m - 3)
            for k in range(2):
                for t in range(2):
                    tr = pe.transpose(PS[4 + m % 4][:, 256 * k + 128 * t:256 * k + 128 * t + 128],
                                      src(2 * n + k, t), ident[:, :])
            tr.then_inc(sem("turned"), 1)

    def turn_high(act, turn, out, scale=None):
        for n in range(turn.tiles // 2):
            m = turn.first + n
            act.wait_ge(sem("turned"), m + 1)
            bank = PS[4 + m % 4]
            if scale is None or scale(2 * n) is None:
                act.activation(out[:, 2 * n:2 * n + 2, :], bank[:, :], ACT.Copy
                               ).then_inc(sem("x_high_made"), 1)
            else:
                act.activation(out[:, 2 * n, :], bank[:, 0:256], ACT.Copy, scale=scale(2 * n))
                act.activation(out[:, 2 * n + 1, :], bank[:, 256:512], ACT.Copy,
                               scale=scale(2 * n + 1)).then_inc(sem("x_high_made"), 1)

    def turn_low(vec, turn, hi, lo, scale=None):
        for n in range(turn.tiles // 2):
            m = turn.first + n
            vec.wait_ge(sem("x_high_made"), turn.first_high + n + 1)
            bank = PS[4 + m % 4]
            if scale is None or scale(2 * n) is None:
                vec.tensor_tensor(lo[:, 2 * n:2 * n + 2, :],
                                  bank[:, :].rearrange("p (k s) -> p k s", k=2),
                                  hi[:, 2 * n:2 * n + 2, :].bitcast(F32), ALU.subtract
                                  ).then_inc(sem("turned_read"), 1)
            else:
                for k in range(2):
                    op = vec.scalar_tensor_tensor(
                        out=lo[:, 2 * n + k, :], in0=bank[:, 256 * k:256 * k + 256],
                        scalar=scale(2 * n + k), in1=hi[:, 2 * n + k, :].bitcast(F32),
                        op0=ALU.mult, op1=ALU.subtract)
                op.then_inc(sem("turned_read"), 1)

    def turned_ready(pe, turn):
        def ready(c, k):
            if c is None:
                pe.wait_ge(sem("turned_read"), turn.first + turn.tiles // 2)
            elif k % 2 == 0:
                pe.wait_ge(sem("turned_read"), turn.first + 2 * c + k // 2 + 1)
        return ready

    class Root:
        count = 0

        def __init__(self, col, width, n, eps):
            self.at = slice(col, col + width)
            self.n, self.eps = n, eps
            self.first = Root.count
            Root.count += 1

    Root.count = 0

    def root_vec_1(vec, r):
        vec.tensor_scalar(stat[:, r.at], stat[:, r.at], 1.0 / r.n, r.eps, ALU.mult, ALU.add
                          ).then_inc(sem("mean_made"), 1)

    def root_act(act, r):
        act.wait_ge(sem("mean_made"), r.first + 1)
        act.activation(stat[:, r.at], stat[:, r.at], ACT.Sqrt).then_inc(sem("root_made"), 1)

    def root_vec_2(vec, r):
        vec.wait_ge(sem("root_made"), r.first + 1)
        vec.reciprocal(stat[:, r.at], stat[:, r.at]).then_inc(sem("inverse_made"), 1)
        vec.wait_ge(sem("inverse_made"), r.first + 1)


    def square_sums(act, src, cols, junk, ready):
        ready()
        for t in range(2):
            op = act.activation(junk[:, t, :] if junk.shape[1] == 2 else junk[:, 0, :], src(t), ACT.Square,
                                accum_out=stat[:, cols + t:cols + t + 1])
            if t == 0 and junk.shape[1] == 1:
                op.then_inc(sem("square_half"), 1)
                SQ.act += 1
                act.wait_ge(sem("square_half"), SQ.act)
        op.then_inc(sem("squares_made"), 1)

    class SQ:
        act = 0

    XR = a["x"].rearrange("o (t p) d -> p (o t) d", p=128)

    def start_act(act):
        act.dma_start(X[:, :, :], XR).then_inc(sem("x_loaded"), 16)
        act.dma_start(ident[:, :], table("ident")).then_inc(sem("start_loaded"), 16)
        for n, (name, rows) in enumerate((("pre_mix_g", 16), ("pre_ffn_g", 16))):
            act.dma_start(vec_in[16 * n:16 * n + 16, :], a[name].rearrange("o (k p) -> (o k) p", p=128)
                          ).then_inc(sem("start_loaded"), 16)
        act.dma_start(vec_in[32:128, :], a["od_mu_2"].rearrange("o i (k p) -> (o i k) p", p=128)
                      ).then_inc(sem("start_loaded"), 16)
        for i in range(3):
            act.dma_start(conv_in[:, i, :], a["conv_w"][0, i, :].rearrange("(k p) -> k p", p=128)
                          ).then_inc(sem("start_loaded"), 16)
        act.dma_start(conv_in[:, 3, :], a["conv_b"][0, :].rearrange("(k p) -> k p", p=128)
                      ).then_inc(sem("start_loaded"), 16)

    def start_pe(pe):
        pe.wait_ge(sem("start_loaded"), 16 * 8)
        pe.transpose(PS[4][:, 0:128], vec_in[:, :], ident[:, :])
        for i in range(4):
            tr = pe.transpose(PS[5][:, 88 * i:88 * i + 88], conv_in[:, i, :], ident[0:88, 0:88])
        tr.then_inc(sem("gains_turned"), 1)
        pe.wait_ge(sem("gains_ready"), 1)

    def start_vec(vec):
        vec.memset(small[:, :], 0.0).then_inc(sem("acc_free"), 2)
        vec.wait_ge(sem("gains_turned"), 1)
        vec.tensor_copy(gains[:, :], PS[4][:, 0:128])
        vec.tensor_copy(conv[:, :, :], PS[5][:, 0:352].rearrange("p (i k) -> p i k", i=4)
                        ).then_inc(sem("gains_ready"), 1)

    xh = at("a_h_high", [128, KT, S], F32R, PH)
    xl = at("a_h_low", [128, KT, S], F32R, PH + 16)
    PJ = at("a_proj", [128, 2, 3840], F32, PH + 56)
    FT = at("a_feature_rows", [128, 22, S], F32, PH + 32)
    KS = at("a_k_swapped", [128, 2, 128], F32, PH + 54)
    FB = [at(f"a_bias{i}", [128, 384], F32, PH + 86 + 1.5 * i) for i in range(4)]
    PR = [at(f"a_probs{i}", [128, 384], F32, PH + 92 + 1.5 * i) for i in range(2)]
    PT = [at(f"a_probs_turned{i}", [128, 384], F32, PH + 95 + 1.5 * i) for i in range(2)]
    TM = at("a_first_map", [128, 2, 128], F32, PH + 98)
    flip = at("a_flip", [128, 128], F32, PH + 99)
    tab = at("a_table", [34, 20], F32, PH + 99.5)
    buckets = at("a_buckets", [34, 384], F32, PH + 100)
    rev = at("a_bias_rows", [20, 384], F32, PH + 101.5)
    lamv = at("a_lambdas", [128, 4, 64], F32, PH + 103)
    sinks = at("a_sinks", [128, 8], F32, PH + 99.625)
    subg = at("a_subln", [128, 1], F32, PH + 99.75)
    XN = at("a_normed", [128, 2, D], F32, PH + 56)
    JK = at("a_squares", [128, 1, D], F32, PH + 104)
    yh = at("a_y_high", [128, 12, S], F32R, PH + 32)
    yl = at("a_y_low", [128, 12, S], F32R, PH + 44)
    GA = at("a_gates", [128, 2, 3 * D], F32, PH + 56)
    BR = [at(f"a_branch{i}", [128, 2, PANEL], F32, PH + 104 + 4 * i) for i in range(2)]
    BG = [at(f"a_gate_bias{i}", [128, PANEL], F32, PH + 112 + 2 * i) for i in range(2)]
    MX = at("a_mix", [128, 2, D], F32, PH)
    mh = at("a_mix_high", [128, KT, S], F32R, PH + 16)
    ml = at("a_mix_low", [128, KT, S], F32R, PH + 32)
    YA = at("a_out", [128, 2, D], F32, PH + 56)
    RA = at("a_out_gain", [128, D], F32, PH + 112)
    bias_rows = dram("bias_rows", [20, 384])

    QKV, GATES = 3840, 3840
    V_COL = {"a": 1024, "b": 2176, "c": 3328}
    if "A" in segments:
        w_in_v = kview(a["w_in"][0])
        add_job("qkv", lambda p: (w_in_v, 0, PANEL * p, PANEL if p < 7 else 256), 8, 4,
                lambda p, c: (xh, xl, 4 * c), 0)
        add_job("gates", lambda p: (w_in_v, 0, ((p if isinstance(p, int) else p[0] * 2 + p[1]) * PANEL) + GATES, PANEL),
                12, 4, lambda p, c: (xh, xl, 4 * c), 2)
        w_branch = [kview(a[n][0]) for n in ("w_oa", "w_ob", "w_oc")]
        add_job("branches", lambda p: (w_branch[p % 3], 0, PANEL * (p // 3), PANEL), 12, 1,
                lambda p, c: (yh, yl, 4 * (p % 3)), 0)
        w_out_v = kview(a["w_out"][0])
        add_job("mix_out", lambda p: (w_out_v, 0, PANEL * p, PANEL), 4, 4,
                lambda p, c: (mh, ml, 4 * c), 0)
        TA_h, TA_f, TA_y, TA_m = Turn(16, True), Turn(22, False), Turn(12, True), Turn(16, True)
        RT_x, RT_sub, RT_mix = Root(0, 2, D, EPS), Root(2, 8, 128, EPS), Root(10, 2, D, EPS)

    def units():
        out = [("a", h, h, m, 4 + h, V_COL["a"] + 128 * h, 128, 128 * h) for h in range(4) for m in range(2)]
        for h in range(8):
            kv = h // 4
            out.append(("b", 4 + h, 8 + h // 2, h % 2, 12 if kv == h % 2 else 13,
                        V_COL["b"] + 64 * kv, 64, 512 + 64 * h))
        out += [("c", 12 + h, 14 + h // 2, h % 2, 18 + h // 2, V_COL["c"] + 64 * h, 64, 1536 + 64 * h)
                for h in range(8)]
        return out

    U = units()
    heads = [u[1] for u in U]
    last_use = {h: max(i for i, u in enumerate(U) if u[1] == h) for h in heads}

    def a_pool(gp):
        gp.dma_start(flip[:, :], table("flip")).then_inc(sem("a_loaded"), 16)
        gp.dma_start(tab[0:32, :], a["rel_bias_table"]).then_inc(sem("a_loaded"), 16)
        gp.dma_start(tab[32:34, :], table("marks")[32:34, :]).then_inc(sem("a_loaded"), 16)
        gp.dma_start(buckets[:, :], table("buckets")[0:34, :]).then_inc(sem("a_loaded"), 16)
        for i, n in enumerate(("lam_q1", "lam_k1", "lam_q2", "lam_k2")):
            gp.dma_start(lamv[:, i, :], a[n][0].partition_broadcast(128)).then_inc(sem("a_loaded"), 16)
        gp.dma_start(sinks[:, :], a["sinks"][0].partition_broadcast(128)).then_inc(sem("a_loaded"), 16)
        gp.dma_start(subg[:, :], a["diff_subln_g"].rearrange("o p -> p o")).then_inc(sem("a_loaded"), 16)
        gp.wait_ge(sem("bias_rows_made"), 1)
        gp.dma_start(bias_rows, rev[:, :]).then_inc(sem("bias_rows_stored"), 16)
        gp.wait_ge(sem("bias_rows_stored"), 16)
        for h in range(20):
            if h >= 4:
                gp.wait_ge(sem("scores"), last_use[h - 4] + 1)
            for q, (c, w) in enumerate(((0, 128), (128, 256))):
                src = bass.AP(tensor=bias_rows.tensor, offset=384 * h + 128 * (1 - q), ap=[[1, 128], [1, w]])
                gp.dma_start(FB[h % 4][:, c:c + w], src).then_inc(sem(f"bias_loaded{h % 4}"), 16)
        j = plan["gates"]
        gp.wait_ge(sem("y_made"), len(U))
        for p in range(12):
            if p >= 2:
                gp.wait_ge(sem("gate_biased"), p - 1)
            gp.dma_start(BG[p % 2][:, :], a["b_gate"][0, PANEL * p:PANEL * p + PANEL].partition_broadcast(128)
                         ).then_inc(sem(f"gate_bias_loaded{p % 2}"), 16)
        gp.wait_ge(sem("gate_biased"), 12)
        gp.dma_start(RA[:, :], a["post_mix_g"][0].partition_broadcast(128)).then_inc(sem("mix_gain_loaded"), 16)

    def ft_source(k, t):
        if k == 13:
            return KS[:, t, :]
        col = 128 * k if k < 8 else 1536 + 128 * (k - 8) if k < 12 else 2048 if k == 12 else 2304 + 128 * (k - 14)
        return PJ[:, t, col:col + 128]

    def a_pe(pe):
        turn_pe(pe, TA_h, lambda k, t: XN[:, t, 128 * k:128 * k + 128], lambda n: pe.wait_ge(sem("x_normed"), 1))
        pe.wait_ge(sem("a_loaded"), 16 * 10)
        pe.matmul(PS[3][0:20, 0:384], tab[:, :], buckets[:, :], start=True, stop=True).then_inc(sem("bias_product"), 1)
        pe.wait_ge(sem("bias_rows_made"), 1)
        run_pe(pe, plan["qkv"], turned_ready(pe, TA_h))
        jq = plan["qkv"]

        def ft_ready(n):
            pe.wait_ge(sem("acc_free"), jq.p0 + jq.panels + 2)
            if n == 6:
                pe.wait_ge(sem("k_swapped"), 1)
        turn_pe(pe, TA_f, ft_source, ft_ready)
        for i in range(len(U) + 2):
            if i < len(U):
                kind, h, qt, half, kt, vc, w, oc = U[i]
                r = slice(64 * half, 64 * half + 64)
                bank = PS[4 + i % 2]
                if i == 0:
                    pe.wait_ge(sem("turned_read"), TA_f.first + 11)
                if i >= 2:
                    pe.wait_ge(sem("probs"), i - 1)
                pe.wait_ge(sem(f"bias_loaded{h % 4}"), 32 * (h // 4 + 1))
                pe.matmul(bank[:, 0:384], flip[:, :], FB[h % 4][:, :], start=True, stop=True)
                pe.matmul(bank[:, 0:128], FT[r, qt, 0:128], FT[r, kt, 0:128], start=False, stop=True,
                          skip_group_check=True)
                pe.matmul(bank[:, 128:384], FT[r, qt, 128:256], FT[r, kt, 0:256], start=False, stop=True,
                          skip_group_check=True).then_inc(sem("scores"), 1)
            if 1 <= i <= len(U):
                n = i - 1
                pe.wait_ge(sem("probs"), n + 1)
                if n >= 2:
                    pe.wait_ge(sem("probs_turned"), n - 1)
                for b in range(3):
                    tr = pe.transpose(PS[6 + n % 2][:, 128 * b:128 * b + 128], PR[n % 2][:, 128 * b:128 * b + 128],
                                      ident[:, :])
                tr.then_inc(sem("probs_transposed"), 1)
            if i >= 2:
                n = i - 2
                kind, h, qt, half, kt, vc, w, oc = U[n]
                pe.wait_ge(sem("probs_turned"), n + 1)
                if n >= 2:
                    pe.wait_ge(sem("y_made"), n - 1)
                bank, pt = PS[n % 2], PT[n % 2]
                pe.matmul(bank[:, 0:w], pt[:, 0:128], PJ[:, 0, vc:vc + w], start=True, stop=True)
                pe.matmul(bank[:, 128:128 + w], pt[:, 128:256], PJ[:, 0, vc:vc + w], start=True, stop=False)
                pe.matmul(bank[:, 128:128 + w], pt[:, 256:384], PJ[:, 1, vc:vc + w], start=False, stop=True
                          ).then_inc(sem("values"), 1)
        def y_ready(n):
            pe.wait_ge(sem("y_made"), len(U))
            pe.wait_ge(sem("y_normed"), 1)
        turn_pe(pe, TA_y, lambda k, t: PJ[:, t, (128 * k if k < 8 else 512 + 128 * k):(128 * k if k < 8 else 512 + 128 * k) + 128],
                y_ready)
        run_pe(pe, plan["gates"])
        run_pe(pe, plan["branches"], lambda c, k: pe.wait_ge(sem("turned_read"), TA_y.first + 6) if k == 0 else None)
        turn_pe(pe, TA_m, lambda k, t: MX[:, t, 128 * k:128 * k + 128],
                lambda n: pe.wait_ge(sem("mix_made"), 3 * (n // 2 + 1)))
        run_pe(pe, plan["mix_out"], turned_ready(pe, TA_m))

    def a_act(act):
        act.wait_ge(sem("x_loaded"), 16)
        square_sums(act, lambda t: X[:, t, :], 0, JK, lambda: None)
        root_act(act, RT_x)
        turn_high(act, TA_h, xh, lambda k: gains[:, k:k + 1])
        act.wait_ge(sem("lam_sums"), 1)
        act.activation(small[:, 34:36], small[:, 32:34], ACT.Exp).then_inc(sem("lam_exps"), 1)
        run_act(act, plan["qkv"], lambda p, t: PJ[:, t, PANEL * p:PANEL * p + (PANEL if p < 7 else 256)])
        for i in range(len(U) + 1):
            if i < len(U):
                kind, h, qt, half, kt, vc, w, oc = U[i]
                act.wait_ge(sem("max_made"), MAXES[i])
                if i >= 2:
                    act.wait_ge(sem("probs_transposed"), i - 1)
                if kind == "b":
                    s = h - 4
                    act.activation(small[:, 48 + 2 * s:50 + 2 * s], nstat[:, 2 * i:2 * i + 2], ACT.Exp,
                                   bias=sinks[:, s:s + 1])
                act.activation(PR[i % 2][:, 0:128], PS[4 + i % 2][:, 0:128], ACT.Exp,
                               bias=nstat[:, 2 * i:2 * i + 1], accum_out=small[:, 64 + 2 * i - 0:65 + 2 * i])
                act.activation(PR[i % 2][:, 128:384], PS[4 + i % 2][:, 128:384], ACT.Exp,
                               bias=nstat[:, 2 * i + 1:2 * i + 2], accum_out=small[:, 65 + 2 * i:66 + 2 * i]
                               ).then_inc(sem("probs"), 1)
            if i >= 1:
                n = i - 1
                act.wait_ge(sem("probs_transposed"), n + 1)
                if n >= 2:
                    act.wait_ge(sem("values"), n - 1)
                act.activation(PT[n % 2][:, :], PS[6 + n % 2][:, 0:384], ACT.Copy).then_inc(sem("probs_turned"), 1)
        for h in range(4):
            for t in range(2):
                act.wait_ge(sem("y_made"), 8)
                n = 2 * h + t
                op = act.activation(JK[:, 0, 128 * n:128 * n + 128], PJ[:, t, 128 * h:128 * h + 128], ACT.Square,
                                    accum_out=stat[:, 2 + 4 * t + h:3 + 4 * t + h])
        op.then_inc(sem("squares_made"), 1)
        root_act(act, RT_sub)
        turn_high(act, TA_y, yh, lambda k: small[:, 36:37] if k < 4 else None)
        run_act(act, plan["gates"], lambda p, t: GA[:, t, bass.ds((p[0] * 2 + p[1]) * PANEL, PANEL)])
        jb = plan["branches"]

        def gate(p):
            n, b = p // 3, p % 3
            col = b * D + n * PANEL
            act.wait_ge(sem("gate_biased"), 12)
            act.activation(GA[:, :, col:col + PANEL], GA[:, :, col:col + PANEL], ACT.Sigmoid)
            if p >= 2:
                act.wait_ge(sem("mix_made"), p - 1)
        run_act(act, jb, lambda p, t: BR[p % 2][:, t, :], free=gate)
        turn_high(act, TA_m, mh)
        run_act(act, plan["mix_out"], lambda p, t: YA[:, t, PANEL * p:PANEL * p + PANEL])
        square_sums(act, lambda t: YA[:, t, :], 10, JK,
                    lambda: act.wait_ge(sem("acc_free"), plan["mix_out"].p0 + 4 + 2))
        root_act(act, RT_mix)

    MAXES = []
    n_max = 0
    for u in U:
        n_max += 2 if u[0] == "b" else 1
        MAXES.append(n_max)

    def a_vec(vec):
        vec.wait_ge(sem("squares_made"), 1)
        root_vec_1(vec, RT_x)
        root_vec_2(vec, RT_x)
        for t in range(2):
            op = vec.tensor_scalar(XN[:, t, :], X[:, t, :], stat[:, t:t + 1], None, ALU.mult)
        op.then_inc(sem("x_normed"), 1)
        turn_low(vec, TA_h, xh, xl, lambda k: gains[:, k:k + 1])
        vec.wait_ge(sem("bias_product"), 1)
        vec.tensor_copy(rev[:, :], PS[3][0:20, 0:384]).then_inc(sem("bias_rows_made"), 1)
        vec.tensor_tensor(lamv[:, 0, :], lamv[:, 0, :], lamv[:, 1, :], ALU.mult)
        vec.tensor_tensor(lamv[:, 2, :], lamv[:, 2, :], lamv[:, 3, :], ALU.mult).then_inc(sem("a_vec"), 1)
        vec.wait_ge(sem("a_vec"), 1)
        vec.tensor_reduce(small[:, 32:34], lamv[:, 0:3:2, :], AX.X, ALU.add).then_inc(sem("lam_sums"), 1)
        vec.tensor_scalar(small[:, 36:37], subg[:, :], 0.8, None, ALU.mult)
        vec.tensor_scalar(small[:, 40:48], sinks[:, :], -1.0, None, ALU.mult)
        vec.wait_ge(sem("lam_exps"), 1)
        vec.scalar_tensor_tensor(out=small[:, 37:38], in0=small[:, 35:36], scalar=-0.2, in1=small[:, 34:35],
                                 op0=ALU.add, op1=ALU.subtract).then_inc(sem("a_vec"), 1)
        vec.wait_ge(sem("a_vec"), 2)
        run_vec(vec, plan["qkv"])
        jq = plan["qkv"]
        vec.wait_ge(sem("acc_free"), jq.p0 + jq.panels + 2)
        vec.tensor_copy(KS[:, :, 0:64], PJ[:, :, 2112:2176])
        vec.tensor_copy(KS[:, :, 64:128], PJ[:, :, 2048:2112]).then_inc(sem("k_swapped"), 1)
        for n in range(11):
            vec.wait_ge(sem("turned"), TA_f.first + n + 1)
            q = n in (0, 1, 4, 5, 7, 8)
            m = TA_f.first + n
            vec.tensor_scalar(FT[:, 2 * n:2 * n + 2, :], PS[4 + m % 4][:, :].rearrange("p (k s) -> p k s", k=2),
                              0.125 if q else 1.0, None, ALU.mult).then_inc(sem("turned_read"), 1)
        nv = 2
        for i in range(len(U) + 2):
            if i < len(U):
                kind, h, qt, half, kt, vc, w, oc = U[i]
                vec.wait_ge(sem("scores"), i + 1)
                vec.tensor_reduce(nstat[:, 2 * i:2 * i + 1], PS[4 + i % 2][:, 0:128], AX.X, ALU.max, negate=True)
                op = vec.tensor_reduce(nstat[:, 2 * i + 1:2 * i + 2], PS[4 + i % 2][:, 128:384], AX.X, ALU.max,
                                       negate=True)
                op.then_inc(sem("max_made"), 1)
                if kind == "b":
                    vec.wait_ge(sem("max_made"), MAXES[i] - 1)
                    vec.tensor_scalar(nstat[:, 2 * i:2 * i + 2], nstat[:, 2 * i:2 * i + 2],
                                      small[:, 40 + h - 4:41 + h - 4], None, ALU.min).then_inc(sem("max_made"), 1)
            if i >= 2:
                n = i - 2
                kind, h, qt, half, kt, vc, w, oc = U[n]
                vec.wait_ge(sem("values"), n + 1)
                sm = small[:, 64 + 2 * n:66 + 2 * n]
                if kind == "b":
                    s = h - 4
                    vec.tensor_tensor(sm, sm, small[:, 48 + 2 * s:50 + 2 * s], ALU.add).then_inc(sem("a_vec"), 1)
                    nv += 1
                    vec.wait_ge(sem("a_vec"), nv)
                vec.reciprocal(sm, sm).then_inc(sem("a_vec"), 1)
                nv += 1
                vec.wait_ge(sem("a_vec"), nv)
                bank = PS[n % 2]
                if kind == "a" and half == 1:
                    vec.tensor_scalar(sm, sm, small[:, 37:38], None, ALU.mult).then_inc(sem("a_vec"), 1)
                    nv += 1
                    vec.wait_ge(sem("a_vec"), nv)
                for t in range(2):
                    src, r = bank[:, 128 * t:128 * t + w], small[:, 64 + 2 * n + t:65 + 2 * n + t]
                    if kind == "a" and half == 0:
                        op = vec.tensor_scalar(TM[:, t, :], src, r, None, ALU.mult)
                    elif kind == "a":
                        op = vec.scalar_tensor_tensor(out=PJ[:, t, oc:oc + w], in0=src, scalar=r, in1=TM[:, t, :],
                                                      op0=ALU.mult, op1=ALU.add)
                    else:
                        op = vec.tensor_scalar(PJ[:, t, oc:oc + w], src, r, None, ALU.mult)
                op.then_inc(sem("y_made"), 1)
                vec.wait_ge(sem("y_made"), n + 1)
        vec.wait_ge(sem("squares_made"), 2)
        root_vec_1(vec, RT_sub)
        root_vec_2(vec, RT_sub)
        ya = PJ[:, :, 0:512].rearrange("p t (h e) -> p t h e", h=4)
        vec.tensor_tensor(ya, ya, stat[:, 2:10].rearrange("p (t h) -> p t h", t=2).unsqueeze(3).to_broadcast([128, 2, 4, 128]),
                          ALU.mult).then_inc(sem("y_normed"), 1)
        turn_low(vec, TA_y, yh, yl, lambda k: small[:, 36:37] if k < 4 else None)
        jg = plan["gates"]

        def bias(p):
            P = panel_number(jg, p)
            vec.wait_ge(sem("acc_free"), P + 3)
            i, q = p
            vec.wait_ge(sem(f"gate_bias_loaded{q}"), i * 16 + 16)
            g = GA[:, :, bass.ds((i * 2 + q) * PANEL, PANEL)]
            vec.tensor_tensor(g, g, BG[q][:, :].unsqueeze(1).to_broadcast([128, 2, PANEL]), ALU.add
                              ).then_inc(sem("gate_biased"), 1)
        run_vec(vec, jg, bias)
        jb = plan["branches"]

        def mix(p):
            n, b = p // 3, p % 3
            vec.wait_ge(sem("acc_free"), jb.p0 + p + 3)
            g = GA[:, :, b * D + n * PANEL:b * D + n * PANEL + PANEL]
            m = MX[:, :, n * PANEL:n * PANEL + PANEL]
            if b == 0:
                vec.tensor_tensor(m, BR[p % 2][:, :, :], g, ALU.mult).then_inc(sem("mix_made"), 1)
            else:
                vec.tensor_tensor(BR[p % 2][:, :, :], BR[p % 2][:, :, :], g, ALU.mult).then_inc(sem("branch_gated"), 1)
                vec.wait_ge(sem("branch_gated"), 2 * n + b)
                vec.wait_ge(sem("mix_made"), p)
                vec.tensor_tensor(m, m, BR[p % 2][:, :, :], ALU.add).then_inc(sem("mix_made"), 1)
        run_vec(vec, jb, mix)
        turn_low(vec, TA_m, mh, ml)
        run_vec(vec, plan["mix_out"])
        vec.wait_ge(sem("squares_made"), 3)
        root_vec_1(vec, RT_mix)
        root_vec_2(vec, RT_mix)
        vec.wait_ge(sem("mix_gain_loaded"), 16)
        add_normed(vec, YA, 10, RA, "mix_added")

    def add_normed(vec, y, col, row, done):
        for t in range(2):
            vec.scalar_tensor_tensor(out=y[:, t, :], in0=y[:, t, :], scalar=stat[:, col + t:col + t + 1],
                                     in1=row[:, :], op0=ALU.mult, op1=ALU.mult).then_inc(sem(done), 1)
        for t in range(2):
            vec.wait_ge(sem(done), t + 1)
            vec.tensor_tensor(X[:, t, :], X[:, t, :], y[:, t, :], ALU.add).then_inc(sem(done), 1)

    OUTR = a["out"].rearrange("o (t p) d -> p (o t) d", p=128)
    last = {"A": ("mix_added", 4), "B": ("ffn_added", 4), "C": ("even_normed", 2), "D": ("odd_normed", 2)}

    segs = {"A": (a_pe, a_act, a_vec, a_pool)}

    bh = at("b_h_high", [128, KT, S], F32R, PH)
    bl = at("b_h_low", [128, KT, S], F32R, PH + 16)
    BN = at("b_normed", [128, 2, D], F32, PH + 48)
    JB = at("b_squares", [128, 1, D], F32, PH + 104)
    fh = at("b_ff_high", [128, FT_TILES, S], F32R, PH + 32)
    fl = at("b_ff_low", [128, FT_TILES, S], F32R, PH + 76)
    UP = [at(f"b_up{q}", [128, 2, PANEL], F32, 64 + 4 * q) for q in range(2)]
    CV = [at(f"b_conv{q}", [128, 4, S], F32, 72 + 4 * q) for q in range(2)]
    CW = at("b_taps", [128, 2, 4, 4], F32, 86.5)
    YB = at("b_out", [128, 2, D], F32, PH)
    RB = at("b_out_gain", [128, D], F32, PH + 16)
    x_kept = dram("x_kept", [S, D])
    XKEPT = x_kept.rearrange("(t p) d -> p t d", p=128)
    if "B" in segments:
        w_up_v, w_down_v = kview(a["w_up"][0]), kview(a["w_down"][0])
        add_job("up", lambda p: (w_up_v, 0, p[0] * PANEL + D_FF * p[1] if not isinstance(p, int) else 0, PANEL),
                22, 4, lambda p, c: (bh, bl, 4 * c), 2)
        add_job("down", lambda p: (w_down_v, 0, PANEL * p, PANEL), 4, 11, lambda p, c: (fh, fl, 4 * c), 0)
        TB_h = Turn(16, True)
        RT_b, RT_f = Root(12, 2, D, EPS), Root(14, 2, D, EPS)
    ROUNDS = 11

    def b_pool(gp):
        gp.wait_ge(sem("mix_added"), 4) if "A" in segments else gp.wait_ge(sem("x_loaded"), 16)
        gp.dma_start(XKEPT, X[:, :, :]).then_inc(sem("x_kept"), 16)
        gp.wait_ge(sem("ff_low_made"), ROUNDS)
        gp.wait_ge(sem("x_kept"), 16)
        gp.dma_start(X[:, :, :], XKEPT).then_inc(sem("x_back"), 16)
        gp.dma_start(RB[:, :], a["post_ffn_g"][0].partition_broadcast(128)).then_inc(sem("ffn_gain_loaded"), 16)

    def b_pe(pe):
        turn_pe(pe, TB_h, lambda k, t: BN[:, t, 128 * k:128 * k + 128], lambda n: pe.wait_ge(sem("b_normed"), 1))
        j = plan["up"]
        turned_ready(pe, TB_h)(None, None)

        def turn_up(i, q, first=False):
            pe.wait_ge(sem("acc_free"), i * 2 + (j.p0 + q + 3))
            for b in range(2):
                if not first:
                    pe.wait_ge(sem("convolved"), i * 4 + (2 * q + b - 3))
                bank = PS[4 + 2 * q + b]
                for k in range(2):
                    for t in range(2):
                        f = 2 * b + k
                        tr = pe.transpose(bank[:, 256 * k + 128 * t:256 * k + 128 * t + 128],
                                          UP[q][:, t, 128 * f:128 * f + 128], ident[:, :])
                tr.then_inc(sem("up_turned"), 1)

        def products(i, q):
            panel_products(pe, j, (i, q), i * 8 + (j.g0 + q * 4), i * 2 + (j.p0 + q))
        products(0, 0)
        products(0, 1)
        turn_up(0, 0, True)
        products(1, 0)
        turn_up(0, 1, True)
        products(1, 1)
        turn_up(1, 0)
        with pe.Fori(2, ROUNDS) as i:
            products(i, 0)
            turn_up(i - 1, 1)
            products(i, 1)
            turn_up(i, 0)
        turn_up(ROUNDS - 1, 1)
        run_pe(pe, plan["down"], lambda c, k: pe.wait_ge(sem("ff_low_made"), c + 1) if k == 0 else None)

    def b_act(act):
        square_sums(act, lambda t: X[:, t, :], 12, JB,
                    lambda: act.wait_ge(sem("mix_added"), 4) if "A" in segments else act.wait_ge(sem("x_loaded"), 16))
        root_act(act, RT_b)
        turn_high(act, TB_h, bh, lambda k: gains[:, 16 + k:17 + k])
        j = plan["up"]
        act.wait_ge(sem("x_kept"), 16)

        def panel(i, q, free):
            splits(act, True, j, q * 4, 4, i) if not isinstance(i, int) else splits(act, True, j, i * 8 + q * 4, 4)
            if free:
                act.wait_ge(sem("up_turned"), i * 4 + (2 * q - 2))
            evacuate(act, j, (i, q), i * 8 + (j.g0 + 4 * q + 4), lambda t: UP[q][:, t, :])

        def last_tap(i, q):
            act.wait_ge(sem("taps_ready"), i * 2 + (q + 1))
            for b in range(2):
                act.wait_ge(sem("up_turned"), i * 4 + (2 * q + b + 1))
                for k in range(2):
                    f = 2 * b + k
                    op = act.activation(CV[q][:, f, :], PS[4 + 2 * q + b][:, 256 * k:256 * k + 256], ACT.Identity,
                                        scale=CW[:, q, 2, f:f + 1], bias=CW[:, q, 3, f:f + 1])
                op.then_inc(sem("last_tap"), 1)

        def gelu(i):
            act.wait_ge(sem("convolved"), i * 4 + 2)
            act.activation(CV[0][:, :, :], CV[0][:, :, :], ACT.Gelu_apprx_tanh).then_inc(sem("gelu_made"), 1)

        def high(i):
            act.wait_ge(sem("ff_made"), i + 1)
            act.activation(fh[:, bass.ds(i * 4, 4), :], CV[1][:, :, :], ACT.Copy).then_inc(sem("ff_high_made"), 1)

        def gate_tap(i, free):
            if free:
                act.wait_ge(sem("ff_made"), i)
            last_tap(i, 0)

        def value_tap(i, free):
            if free:
                act.wait_ge(sem("ff_low_made"), i)
            last_tap(i, 1)
        panel(0, 0, False)
        panel(0, 1, False)
        gate_tap(0, False)
        panel(1, 0, True)
        value_tap(0, False)
        gelu(0)
        panel(1, 1, True)
        high(0)
        gate_tap(1, True)
        with act.Fori(2, ROUNDS) as i:
            panel(i, 0, True)
            value_tap(i - 1, True)
            gelu(i - 1)
            panel(i, 1, True)
            high(i - 1)
            gate_tap(i, True)
        value_tap(ROUNDS - 1, True)
        gelu(ROUNDS - 1)
        high(ROUNDS - 1)
        jd = plan["down"]
        run_act(act, jd, lambda p, t: YB[:, t, PANEL * p:PANEL * p + PANEL])
        square_sums(act, lambda t: YB[:, t, :], 14, JB2, lambda: act.wait_ge(sem("acc_free"), jd.p0 + 4 + 2))
        root_act(act, RT_f)

    JB2 = at("b_squares_out", [128, 1, D], F32, PH + 24)

    def b_vec(vec):
        vec.wait_ge(sem("squares_made"), SQB)
        root_vec_1(vec, RT_b)
        root_vec_2(vec, RT_b)
        for t in range(2):
            op = vec.tensor_scalar(BN[:, t, :], X[:, t, :], stat[:, 12 + t:13 + t], None, ALU.mult)
        op.then_inc(sem("b_normed"), 1)
        turn_low(vec, TB_h, bh, bl, lambda k: gains[:, 16 + k:17 + k])
        j = plan["up"]

        def panel(i, q, first=0, count=4):
            at = q * 4 + first
            splits(vec, False, j, at, count, i) if not isinstance(i, int) else splits(vec, False, j, i * 8 + at, count)

        def taps(i, q, free):
            if free:
                vec.wait_ge(sem("last_tap"), i * 4 + (2 * q - 2))
            src = conv[:, :, bass.ds(i * 4 + 44 * q, 4)]
            vec.tensor_copy(CW[:, q, :, :], src).then_inc(sem("taps_ready"), 1)
            vec.wait_ge(sem("taps_ready"), i * 2 + (q + 1))

        def older_taps(i, q, between=None):
            for b in range(2):
                if b and between:
                    between()
                vec.wait_ge(sem("last_tap"), i * 4 + (2 * q + b + 1))
                for k in range(2):
                    f = 2 * b + k
                    for lag in (1, 2):
                        src = PS[4 + 2 * q + b][:, 256 * k:256 * k + 256 - lag]
                        c = CV[q][:, f, lag:256]
                        op = vec.scalar_tensor_tensor(out=c, in0=src, scalar=CW[:, q, 2 - lag, f:f + 1], in1=c,
                                                      op0=ALU.mult, op1=ALU.add)
                        if lag == 1:
                            op.then_inc(sem("tap_added"), 1)
                            vec.wait_ge(sem("tap_added"), i * 8 + (4 * q + f + 1))
                op.then_inc(sem("convolved"), 1)

        def product(i):
            vec.wait_ge(sem("gelu_made"), i + 1)
            vec.wait_ge(sem("convolved"), i * 4 + 4)
            vec.tensor_tensor(CV[1][:, :, :], CV[1][:, :, :], CV[0][:, :, :], ALU.mult).then_inc(sem("ff_made"), 1)

        def low(i):
            vec.wait_ge(sem("ff_high_made"), i + 1)
            vec.tensor_tensor(fl[:, bass.ds(i * 4, 4), :], CV[1][:, :, :], fh[:, bass.ds(i * 4, 4), :].bitcast(F32),
                              ALU.subtract).then_inc(sem("ff_low_made"), 1)

        def gate(i, free, between=None):
            taps(i, 0, free)
            older_taps(i, 0, between)

        def value(i, free, between=None):
            taps(i, 1, free)
            older_taps(i, 1, between)
            product(i)
        panel(0, 0)
        panel(0, 1)
        gate(0, False)
        panel(1, 0)
        value(0, False)
        panel(1, 1)
        low(0)
        gate(1, True)
        with vec.Fori(2, ROUNDS) as i:
            panel(i, 0)
            taps(i - 1, 1, True)
            older_taps(i - 1, 1)
            panel(i, 1, 0, 1)
            product(i - 1)
            panel(i, 1, 1, 3)
            low(i - 1)
            gate(i, True)
        value(ROUNDS - 1, True)
        low(ROUNDS - 1)
        run_vec(vec, plan["down"])
        vec.wait_ge(sem("squares_made"), SQB + 1)
        root_vec_1(vec, RT_f)
        root_vec_2(vec, RT_f)
        vec.wait_ge(sem("ffn_gain_loaded"), 16)
        vec.wait_ge(sem("x_back"), 16)
        add_normed(vec, YB, 14, RB, "ffn_added")

    SQB = 4 if "A" in segments else 1

    ch = at("c_x_high", [128, KT, S], F32R, PH)
    cl = at("c_x_low", [128, KT, S], F32R, PH + 16)
    PC = at("c_proj", [128, 2, 6144], F32, PH + 32)
    FC = at("c_feature_rows", [128, 16, S], F32, PH + 80)
    SP = [at(f"c_softplus{i}", [128, 384], F32, PH + 96 + 1.5 * i) for i in range(2)]
    TC = [at(f"c_log{i}", [128, 384], F32, PH + 99 + 1.5 * i) for i in range(2)]
    WT = [at(f"c_weights{i}", [128, 384], F32, PH + 102 + 1.5 * i) for i in range(2)]
    pools = at("c_pool_tables", [128, 4, 384], F32, PH + 105)
    prow = at("c_pool_scale", [128, 1024], F32, PH + 111)
    suffix = at("c_suffix", [128, 128], F32, PH + 115)
    m_ones = at("c_minus_ones", [128, 128], F32, PH + 115.5)
    before = at("c_before", [128, 128], F32, PH + 116)
    hidden = at("c_hidden", [128, 128], F32, PH + 116.5)
    PL = at("c_pooled", [128, 8, S], F32, PH + 80)
    WP = at("c_pool_weights", [128, 2, 4, 256], F32, PH + 88)
    YC = at("c_out", [128, 2, D], F32, PH + 80)
    LN = at("c_norm_rows", [128, 2, D], F32, PH + 96)
    if "C" in segments:
        w_ev = kview(a["ev_w_in_2"][0])
        add_job("even_in", lambda p: (w_ev, 0, (p if isinstance(p, int) else p[0] * 2 + p[1]) * PANEL, PANEL),
                12, 4, lambda p, c: (ch, cl, 4 * c), 2)
        w_eo = kview(a["ev_w_out_2"][0])
        add_job("even_out", lambda p: (w_eo, 0, PANEL * p, PANEL), 4, 4, lambda p, c: (ch, cl, 4 * c), 0)
        TC_x, TC_f, TC_m = Turn(16, True), Turn(16, False), Turn(16, True)

    def diagonal(x):
        return x[:, :].rearrange("p (b s) -> p b s", b=3)[:, 0:3:2, :]

    def c_ready(e):
        if "B" in segments:
            e.wait_ge(sem("ffn_added"), 4)
        else:
            e.wait_ge(sem("x_loaded"), 16)

    def c_pool(gp):
        c_ready(gp)
        for g in range(4):
            gp.dma_start(pools[:, g, 0:256], table(f"pool{g}a")).then_inc(sem("c_loaded"), 16)
            gp.dma_start(pools[:, g, 256:384], table(f"pool{g}b")).then_inc(sem("c_loaded"), 16)
        gp.dma_start(prow[:, :], a["ev_pool_scale_2"][0].partition_broadcast(128)).then_inc(sem("c_loaded"), 16)
        gp.dma_start(suffix[:, :], table("suffix")).then_inc(sem("c_loaded"), 16)
        gp.dma_start(m_ones[:, :], table("minus_ones")).then_inc(sem("c_loaded"), 16)
        gp.dma_start(before[:, :], table("before")).then_inc(sem("c_loaded"), 16)
        gp.dma_start(hidden[:, :], table("hidden")).then_inc(sem("c_loaded"), 16)
        gp.wait_ge(sem("stick_values"), 8)
        for g in range(4):
            gp.dma_start(WP[:, :, g, :], a["ev_w_pool_2"][0, g].rearrange("(k p) n -> p k n", p=128)
                         ).then_inc(sem("pool_weights_loaded"), 16)
        gp.wait_ge(sem("mixed_made"), 12)
        for i, n in enumerate(("ln_g_2", "ln_b_2")):
            gp.dma_start(LN[:, i, :], a[n][0].partition_broadcast(128)).then_inc(sem("c_norm_loaded"), 16)

    def c_pe(pe):
        turn_pe(pe, TC_x, lambda k, t: X[:, t, 128 * k:128 * k + 128], lambda n: c_ready(pe))
        run_pe(pe, plan["even_in"], turned_ready(pe, TC_x))
        j = plan["even_in"]
        turn_pe(pe, TC_f, lambda k, t: PC[:, t, 128 * k:128 * k + 128],
                lambda n: pe.wait_ge(sem("acc_free"), j.p0 + j.panels + 2))
        pe.wait_ge(sem("turned_read"), TC_f.first + 8)
        pe.wait_ge(sem("c_loaded"), 16 * 13)
        for i in range(8 + 2):
            if i < 8:
                h = i
                bank = PS[4 + i % 2]
                if i >= 2:
                    pe.wait_ge(sem("stick_exp"), i - 1)
                pe.matmul(bank[:, 0:256], FC[:, 8 + h, 0:128], FC[:, h, :], start=True, stop=True)
                pe.matmul(bank[:, 256:384], FC[:, 8 + h, 128:256], FC[:, h, 128:256], start=False, stop=True,
                          skip_group_check=True).then_inc(sem("stick_scores"), 1)
            if 1 <= i <= 8:
                n = i - 1
                bank, sp = PS[4 + n % 2], SP[n % 2]
                pe.wait_ge(sem("softplus_masked"), n + 1)
                pe.matmul(bank[:, 0:384], suffix[:, :], sp[:, :], start=False, stop=True, skip_group_check=True)
                pe.matmul(diagonal(bank[:, 0:384]), ident[:, :], hidden[:, :].unsqueeze(1).to_broadcast([128, 2, 128]),
                          start=False, stop=True, skip_group_check=True)
                pe.matmul(bank[:, 128:256], m_ones[:, :], sp[:, 256:384], start=False, stop=True,
                          skip_group_check=True).then_inc(sem("stick_logs"), 1)
            if i >= 2:
                n = i - 2
                bank, w = PS[6 + n % 2], WT[n % 2]
                pe.wait_ge(sem("stick_exp"), n + 1)
                if n >= 2:
                    pe.wait_ge(sem("mixed_made"), n - 1)
                v = [PC[:, t, 2048 + 128 * n:2048 + 128 * n + 128] for t in range(2)]
                pe.matmul(bank[:, 0:128], w[:, 0:128], v[0], start=True, stop=True)
                pe.matmul(bank[:, 128:256], w[:, 128:256], v[0], start=True, stop=False)
                pe.matmul(bank[:, 128:256], w[:, 256:384], v[1], start=False, stop=True
                          ).then_inc(sem("stick_values"), 1)
        for g in range(4):
            bank = PS[g]
            for k in range(2):
                c = 4096 + 256 * g + 128 * k
                pe.matmul(bank[:, 256 * k:256 * k + 256], PC[:, 0, c:c + 128], pools[:, g, 0:256],
                          start=(k == 0), stop=True, skip_group_check=True)
                mm = pe.matmul(bank[:, 256 * k + 128:256 * k + 256], PC[:, 1, c:c + 128], pools[:, g, 256:384],
                               start=False, stop=True, skip_group_check=True)
            mm.then_inc(sem("pool_sums"), 1)
        pe.wait_ge(sem("pool_weights_loaded"), 64)
        for g in range(4):
            bank = PS[4 + g]
            pe.wait_ge(sem("pooled"), g + 1)
            if g == 0:
                pe.wait_ge(sem("mixed_made"), 8)
                pe.wait_ge(sem("stick_exp"), 8)
            for t in range(2):
                for k in range(2):
                    mm = pe.matmul(bank[:, 256 * t:256 * t + 256], PL[:, 2 * g + k, 128 * t:128 * t + 128],
                                   WP[:, k, g, :], start=(k == 0), stop=(k == 1))
            mm.then_inc(sem("pool_products"), 1)
        turn_pe(pe, TC_m, lambda k, t: PC[:, t, 128 * k:128 * k + 128], lambda n: pe.wait_ge(sem("mixed_made"), 12))
        run_pe(pe, plan["even_out"], turned_ready(pe, TC_m))

    def c_act(act):
        turn_high(act, TC_x, ch)
        j = plan["even_in"]
        run_act(act, j, lambda p, t: PC[:, t, bass.ds((p[0] * 2 + p[1]) * PANEL, PANEL)])
        act.wait_ge(sem("acc_free"), j.p0 + j.panels + 2)
        act.activation(PC[:, :, 3072:4096], PC[:, :, 3072:4096], ACT.Silu)
        act.activation(PC[:, :, 5120:6144], PC[:, :, 5120:6144], ACT.Silu).then_inc(sem("silu_made"), 1)
        for i in range(8 + 1):
            if i < 8:
                t = TC[i % 2]
                act.wait_ge(sem("stick_scores"), i + 1)
                if i >= 2:
                    act.wait_ge(sem("softplus_made"), i - 1)
                act.activation(t[:, :], PS[4 + i % 2][:, 0:384], ACT.Abs).then_inc(sem("softplus_parts"), 1)
                act.wait_ge(sem("softplus_parts"), 3 * i + 1)
                act.activation(t[:, :], t[:, :], ACT.Exp, scale=-1.0).then_inc(sem("softplus_parts"), 1)
                act.wait_ge(sem("softplus_parts"), 3 * i + 2)
                act.activation(t[:, :], t[:, :], ACT.Ln, bias=1.0).then_inc(sem("softplus_parts"), 1)
            if i >= 1:
                n = i - 1
                act.wait_ge(sem("stick_logs"), n + 1)
                if n >= 2:
                    act.wait_ge(sem("stick_values"), n - 1)
                act.activation(WT[n % 2][:, :], PS[4 + n % 2][:, 0:384], ACT.Exp).then_inc(sem("stick_exp"), 1)
        turn_high(act, TC_m, ch)
        run_act(act, plan["even_out"], lambda p, t: YC[:, t, PANEL * p:PANEL * p + PANEL])
        norm_act(act, 0)

    def c_vec(vec):
        turn_low(vec, TC_x, ch, cl)
        run_vec(vec, plan["even_in"])
        for n in range(8):
            m = TC_f.first + n
            vec.wait_ge(sem("turned"), m + 1)
            vec.tensor_scalar(FC[:, 2 * n:2 * n + 2, :], PS[4 + m % 4][:, :].rearrange("p (k s) -> p k s", k=2),
                              128 ** -0.5 if n < 4 else 1.0, None, ALU.mult).then_inc(sem("turned_read"), 1)
        vec.wait_ge(sem("silu_made"), 1)
        vec.wait_ge(sem("c_loaded"), 16 * 13)
        mask = before[:, :].unsqueeze(1).to_broadcast([128, 2, 128])
        for i in range(8 + 2):
            if i < 8:
                sp = SP[i % 2]
                vec.wait_ge(sem("softplus_parts"), 3 * i + 3)
                if i >= 2:
                    vec.wait_ge(sem("stick_logs"), i - 1)
                vec.scalar_tensor_tensor(out=sp[:, :], in0=PS[4 + i % 2][:, 0:384], scalar=0.0, in1=TC[i % 2][:, :],
                                         op0=ALU.max, op1=ALU.add).then_inc(sem("softplus_made"), 1)
                vec.wait_ge(sem("softplus_made"), i + 1)
                vec.tensor_tensor(diagonal(sp), diagonal(sp), mask, ALU.mult).then_inc(sem("softplus_masked"), 1)
            if i >= 2:
                n = i - 2
                vec.wait_ge(sem("stick_values"), n + 1)
                vec.tensor_tensor(PC[:, :, 128 * n:128 * n + 128], PS[6 + n % 2][:, 0:256].rearrange("p (t e) -> p t e", t=2),
                                  PC[:, :, 3072 + 128 * n:3072 + 128 * n + 128], ALU.mult).then_inc(sem("mixed_made"), 1)
        for g in range(4):
            vec.wait_ge(sem("pool_sums"), g + 1)
            vec.tensor_copy(PL[:, 2 * g:2 * g + 2, :], PS[g][:, :].rearrange("p (k s) -> p k s", k=2)
                            ).then_inc(sem("pooled"), 1)
        for g in range(4):
            vec.wait_ge(sem("pool_products"), g + 1)
            m = PC[:, :, 1024 + 256 * g:1024 + 256 * g + 256]
            vec.tensor_tensor(m, PS[4 + g][:, :].rearrange("p (t n) -> p t n", t=2),
                              prow[:, 256 * g:256 * g + 256].unsqueeze(1).to_broadcast([128, 2, 256]), ALU.mult
                              ).then_inc(sem("pool_scaled"), 1)
            vec.wait_ge(sem("pool_scaled"), g + 1)
            vec.tensor_tensor(m, m, PC[:, :, 5120 + 256 * g:5120 + 256 * g + 256], ALU.mult).then_inc(sem("mixed_made"), 1)
        turn_low(vec, TC_m, ch, cl)
        run_vec(vec, plan["even_out"])
        norm_vec(vec, YC, LN, "c_norm_loaded", plan["even_out"], "even_normed", 0)

    NORMS = {}

    def norm_act(act, n):
        n = n if "C" in segments else 0
        act.wait_ge(sem("variance_ready"), n + 1)
        act.activation(nstat[:, 94:96], nstat[:, 94:96], ACT.Sqrt).then_inc(sem("deviation_made"), 1)

    def norm_vec(vec, y, rows, loaded, job, done, n):
        n = n if "C" in segments else 0
        steps = [9 * n]

        def step(op):
            steps[0] += 1
            op.then_inc(sem("norm_step"), 1)

        def behind(k=0):
            vec.wait_ge(sem("norm_step"), steps[0] - k)
        vec.wait_ge(sem("acc_free"), job.p0 + job.panels + 2)
        for t in range(2):
            step(vec.scalar_tensor_tensor(out=X[:, t, :], in0=X[:, t, :], scalar=ALPHA, in1=y[:, t, :],
                                          op0=ALU.mult, op1=ALU.add))
        for t in range(2):
            behind(1) if t == 0 else behind(0)
            for c in range(4):
                op = vec.bn_stats(small[:, 24 * t + 6 * c:24 * t + 6 * c + 6], X[:, t, PANEL * c:PANEL * c + PANEL])
        step(op)
        behind()
        for t in range(2):
            op = vec.bn_aggr(small[:, 48 + 2 * t:50 + 2 * t],
                             small[:, 24 * t:24 * t + 24])
        step(op)
        behind()
        vec.tensor_scalar(nstat[:, 94:96], small[:, 49:52:2], LN_EPS, None, ALU.add).then_inc(sem("variance_ready"), 1)
        vec.wait_ge(sem("deviation_made"), n + 1)
        step(vec.reciprocal(small[:, 52:54], nstat[:, 94:96]))
        behind()
        for t in range(2):
            step(vec.tensor_scalar(X[:, t, :], X[:, t, :], small[:, 48 + 2 * t:49 + 2 * t], small[:, 52 + t:53 + t],
                                   ALU.subtract, ALU.mult))
        vec.wait_ge(sem(loaded), 32)
        for i, f in enumerate((ALU.mult, ALU.add)):
            for t in range(2):
                behind(1 if i == 0 or t == 0 else 0)
                op = vec.tensor_tensor(X[:, t, :], X[:, t, :], rows[:, i, :], f)
                if i == 0:
                    step(op)
                else:
                    op.then_inc(sem(done), 1)
            
    segs["B"] = (b_pe, b_act, b_vec, b_pool)
    segs["C"] = (c_pe, c_act, c_vec, c_pool)

    xT = at("d_x", [128, KT, S], F32, PH)
    xx = at("d_shift", [128, KT, S], F32, PH + 16)
    MT = at("d_mixed", [128, KT, S], F32, PH + 32)
    dh = [at(f"d_high{i}", [128, KT, S], F32R, PH + 48 + 32 * i) for i in range(2)]
    dl = [at(f"d_low{i}", [128, KT, S], F32R, PH + 64 + 32 * i) for i in range(2)]
    DS = [at(f"d_staged{i}", [128, 2, PANEL], F32, PH + 112 + 4 * i) for i in range(2)]
    LW = [at(f"d_lora_in{i}", [128, KT, LORA], F32, PH + 80 + 6 * i) for i in range(2)]
    TH = at("d_lora", [LORA, 2, S], F32, 84)
    GW = 256
    GROUPS = D // GW
    RKVG = [[at(f"d_{n}{i}", [128, 2, GW], F32, (PH, PH + 8, 0)[i] + 2 * k) for k, n in enumerate("rkvg")]
            for i in range(3)]
    ROWS = [at(f"d_rows{i}", [128, 5, GW], F32, PH + 16 + 5 * i) for i in range(2)]
    GN_ROWS = [at(f"d_norm_rows_of{i}", [128, 2, GW], F32, (PH + 26, PH + 28, 8)[i]) for i in range(3)]
    ROW_NAMES = ("od_w0_2", "od_a0_2", "od_k_k_2", "od_k_a_2", "od_r_k_2", "od_gn_w_2", "od_gn_b_2")
    W0, A0, KK, KA, RK, GNW, GNB = range(7)
    W2 = [at(f"d_lora_out{i}", [LORA, 2, GW], F32, PH + 30 + 2 * i) for i in range(2)]
    KH = [at(f"d_key{i}", [128, 2, GW], F32, PH + 34 + 2 * i) for i in range(2)]
    NEG_B = [at(f"d_minus_b{i}", [128, 2, GW], F32, PH + 38 + 2 * i) for i in range(2)]
    FR = [at(f"d_feature_rows{i}", [128, 4, 512], F32, PH + 42 + 8 * i) for i in range(2)]
    MBK = [at(f"d_products{i}", [128, 2, 2, 4, 256], F32, (PH + 58, 16)[i]) for i in range(2)]
    MB, MK = [[[MBK[i][:, kind, t, :, :] for t in range(2)] for i in range(2)] for kind in range(2)]
    tk, tw, ta, tq, tr, te, tn, tb = [at(f"d_t{i}", [128, 2, GW], F32, PH + 74 + 2 * i) for i in range(8)]
    XI = [at(f"d_inverse{t}", [128, 4, 128], F32, PH + 90 + 2 * t) for t in range(2)]
    XT = [[at(f"d_inverse_turned{i}{t}", [128, 4, 128], F32, (PH + 94, 10)[i] + 2 * t) for t in range(2)]
          for i in range(2)]
    YI = [at(f"d_step{t}", [128, 4, 128], F32, PH + 98 + 2 * t) for t in range(2)]
    DR = [at(f"d_right{t}", [128, 4, 64], F32, PH + 102 + t) for t in range(2)]
    SA = [at(f"d_removed{t}", [128, 4, 64], F32, PH + 104 + t) for t in range(2)]
    OO = at("d_o", [128, 2, GW], F32, PH + 106)
    P1 = at("d_p1", [128, 2, GW], F32, PH + 108)
    P2 = at("d_p2", [128, 2, GW], F32, PH + 110)
    U0 = at("d_state", [128, 2, 128], F32, 86)
    D_TABLES = 11 * 128 + 2
    d_tables = at("d_tables", [128, D_TABLES], F32, PH + 112.5)
    lev = d_tables[:, 0:7 * 128].rearrange("p (k s) -> p k s", k=7)
    lev0t = d_tables[:, 7 * 128:8 * 128]
    both = d_tables[:, 8 * 128:10 * 128]
    centred = d_tables[:, 10 * 128:11 * 128]
    halves = d_tables[:, 11 * 128:D_TABLES]
    DSM = at("d_small", [128, 3, 64], F32, PH + 118.5)
    OT = at("d_gated", [128, 2, D], F32, 64)
    oh = at("d_o_high", [128, KT, S], F32R, PH + 42)
    ol = at("d_o_low", [128, KT, S], F32R, PH + 58)
    YD = at("d_out", [128, 2, D], F32, PH)
    LD = at("d_norm_rows", [128, 2, D], F32, PH + 16)
    x_kept2 = dram("x_kept2", [S, D])
    XKEPT2 = x_kept2.rearrange("(t p) d -> p t d", p=128)
    kept = dram("rkvg", [4, S, D])
    C = math.exp(-0.5)
    if "D" in segments:
        for n, (name, w) in enumerate((("r", "od_w_r_2"), ("k", "od_w_k_2"), ("v", "od_w_v_2"), ("g", "od_w_g_2"))):
            wv = kview(a[w][0])
            add_job("odd_" + name, (lambda wv: lambda p: (wv, 0, PANEL * p, PANEL))(wv), 4, 4,
                    (lambda n: lambda p, c: (dh[n % 2], dl[n % 2], 4 * c))(n), 0)
        w_oo = kview(a["od_w_o_2"][0])
        add_job("odd_out", lambda p: (w_oo, 0, PANEL * p, PANEL), 4, 4, lambda p, c: (oh, ol, 4 * c), 0)
        TD_x, TD_o = Turn(16, False), Turn(16, True)

    STEPS = {
        "prep_pe": ["lora", "sums", "turn0", "turn1", "turn2", "turn3"],
        "prep_act": ["sigmoids", "squares", "root", "growth", "state_decay", "before", "turned0", "turned1", "turned2",
                     "turned3"],
        "prep_pool": ["kk", "u", "r", "k", "rk", "rkr"],
        "prep_vec": ["lora_w", "lora_a", "norm_sum", "norm_floor", "norm_inverse", "kk", "a1", "k_new", "cs_before",
                     "b", "a", "bonus_sum"],
        "score_pe": [str(j) for j in range(8)],
        "score_vec": [str(j) for j in range(8)],
        "level_pe": ["0Y0", "0Y1"] + [f"{k}{s}{t}" for k in range(1, 7) for s in "YZ" for t in range(2)],
        "level_vec": [f"0{s}{t}" for t in range(2) for s in "YX"] + [
            x for k in range(1, 7) for x in (f"{k}Y0", f"{k}Y1", *([f"{k}X0"] if k < 6 else []), f"{k}T0",
                                             *([f"{k}X1"] if k < 6 else []), f"{k}T1")],
        "level_pool": ["m0", "T0", "m1", "T1"],
        "state_pe": ["d0", "s0", "u", "o0", "d1", "s1", "o1"],
        "state_act": ["d0", "s0", "d1", "s1", "o"],
        "state_vec": ["u0", "u1"],
        "post_act": ["silu", "squares", "root"],
        "post_vec": ["sum", "mean", "centre", "var", "eps", "inverse", "norm"],
        "post_pool": ["bonus", "gain", "bias", "with_bonus", "out"],
    }

    def mark(section, step, n):
        return n * len(STEPS[section]) + (STEPS[section].index(step) + 1)

    def await_step(eng, section, step, n):
        eng.wait_ge(sem(section), mark(section, step, n))

    def by_head(x):
        return x[:, :, :].rearrange("p t (h e) -> p (t h) e", e=64)

    def wide(col, n=64):
        return col.unsqueeze(2).to_broadcast([128, 8, n])

    def row(n, i):
        r = ROWS[n % 2][:, i, :] if i < GNW else GN_ROWS[n % 3][:, i - GNW, :]
        return r.unsqueeze(1).to_broadcast([128, 2, GW])

    def group_loads(sp):
        for par in range(2):
            sp.wait_ge(sem(f"rkvg_stored{par}"), 16 * 8)
        sp.wait_ge(sem("w_low_made"), plan["odd_out"].g0 + 2)
        for n in range(GROUPS):
            if n >= 3:
                await_step(sp, "post_pool", "out", n - 3)
            for k in range(4):
                sp.dma_start(RKVG[n % 3][k][:, :, :],
                             kept[k].rearrange("(t p) d -> p t d", p=128)[:, :, GW * n:GW * n + GW]
                             ).then_inc(sem(f"group_loaded{n % 3}"), 16)
            if n >= 2:
                await_step(sp, "prep_vec", "bonus_sum", n - 2)
            for k, name in enumerate(ROW_NAMES):
                src = a[name][0].rearrange("h e -> (h e)") if name == "od_r_k_2" else a[name][0]
                sp.dma_start(ROWS[n % 2][:, k, :] if k < GNW else GN_ROWS[n % 3][:, k - GNW, :], src[GW * n:GW * n + GW].partition_broadcast(128)
                             ).then_inc(sem(f"group_loaded{n % 3}"), 16)
            if n >= 2:
                await_step(sp, "prep_pe", "lora", n - 2)
            for k, name in enumerate(("od_w2_2", "od_a2_2")):
                sp.dma_start(W2[n % 2][:, k, :], a[name][0][:, GW * n:GW * n + GW]
                             ).then_inc(sem(f"group_loaded{n % 3}"), 16)

    def loaded(eng, n):
        eng.wait_ge(sem(f"group_loaded{n % 3}"), 16 * 13 * (n // 3 + 1))

    def prep_pe(pe, n, part):
        par = n % 2
        if part == 1:
            loaded(pe, n)
            if n >= 1:
                await_step(pe, "score_vec", "7", n - 1)
            for i in range(2):
                for t in range(2):
                    mm = pe.matmul(PS[6 + i][:, GW * t:GW * t + GW], TH[:, i, 128 * t:128 * t + 128], W2[n % 2][:, i, :],
                                   start=True, stop=True)
            mm.then_inc(sem("prep_pe"), 1)
        if part == 2:
            await_step(pe, "prep_act", "sigmoids", n)
            for t in range(2):
                pe.matmul(PS[6][:, GW * t:GW * t + GW], centred[:, :], tw[:, t, :], start=True, stop=True)
            for p in range(2):
                pe.matmul(PS[7][:, p:p + 1], tw[:, 0, 128 * p:128 * p + 128], halves[:, 0:1], start=True, stop=False)
                mm = pe.matmul(PS[7][:, p:p + 1], tw[:, 1, 128 * p:128 * p + 128], halves[:, 1:2], start=False, stop=True)
            mm.then_inc(sem("prep_pe"), 1)
        if part in (5, 6):
            if part == 5:
                await_step(pe, "prep_vec", "a", n)
                await_step(pe, "prep_pool", "k", n)
                await_step(pe, "prep_act", "state_decay", n)
            for j in (0, 1) if part == 5 else (2, 3):
                if j >= 2:
                    await_step(pe, "prep_act", f"turned{j - 2}", n)
                t, p = j // 2, j % 2
                for q, src in enumerate((tq, tr, NEG_B[par], KH[par])):
                    tr_ = pe.transpose(PS[6 + j % 2][:, 128 * q:128 * q + 128], src[:, t, 128 * p:128 * p + 128],
                                       ident[:, :])
                tr_.then_inc(sem("prep_pe"), 1)

    def prep_act(act, n, part):
        par = n % 2
        inc = lambda op: op.then_inc(sem("prep_act"), 1)
        if part == 1:
            await_step(act, "prep_vec", "lora_a", n)
            act.activation(tw[:, :, :], tw[:, :, :], ACT.Sigmoid)
            inc(act.activation(ta[:, :, :], ta[:, :, :], ACT.Sigmoid))
            await_step(act, "prep_pool", "kk", n)
            if n >= 1:
                await_step(act, "prep_pe", "turn3", n - 1)
            inc(act.activation(tq[:, :, :], tk[:, :, :], ACT.Square))
        if part == 2:
            await_step(act, "prep_vec", "norm_sum", n)
            inc(act.activation(DSM[:, n % 3, 0:8], DSM[:, n % 3, 0:8], ACT.Sqrt))
        if part == 3:
            await_step(act, "prep_pe", "sums", n)
            cs = PS[6][:, :].rearrange("p (t n) -> p t n", t=2)
            act.activation(tr[:, :, :], cs, ACT.Exp, scale=-C)
            inc(act.activation(te[:, :, :], cs, ACT.Exp, scale=C))
            inc(act.activation(DSM[:, n % 3, 8:10], PS[7][:, 0:2], ACT.Exp, scale=-C))
            await_step(act, "prep_vec", "cs_before", n)
            inc(act.activation(tq[:, :, :], tq[:, :, :], ACT.Exp, scale=-C))
        if part in (5, 6):
            for j in (0, 1) if part == 5 else (2, 3):
                await_step(act, "prep_pe", f"turn{j}", n)
                inc(act.activation(FR[par][:, j, :], PS[6 + j % 2][:, :], ACT.Copy))

    def prep_pool(gp, n, part):
        par = n % 2
        inc = lambda op: op.then_inc(sem("prep_pool"), 1)
        r, k, v, g = RKVG[n % 3]
        if part == 1:
            loaded(gp, n)
            if n >= 1:
                await_step(gp, "prep_vec", "bonus_sum", n - 1)
            inc(gp.tensor_tensor(tk[:, :, :], k[:, :, :], row(n, KK), ALU.mult))
        if part == 3:
            await_step(gp, "prep_vec", "a1", n)
            inc(gp.tensor_tensor(ta[:, :, :], tk[:, :, :], ta[:, :, :], ALU.mult))
            await_step(gp, "prep_act", "growth", n)
            inc(gp.tensor_tensor(tr[:, :, :], r[:, :, :], tr[:, :, :], ALU.mult))
            await_step(gp, "prep_vec", "k_new", n)
            inc(gp.tensor_tensor(KH[par][:, :, :], tn[:, :, :], te[:, :, :], ALU.mult))
        if part == 4:
            inc(gp.tensor_tensor(tb[:, :, :], r[:, :, :], tn[:, :, :], ALU.mult))
            await_step(gp, "prep_pool", "rk", n)
            inc(gp.tensor_tensor(tb[:, :, :], tb[:, :, :], row(n, RK), ALU.mult))

    def prep_vec(vec, n, part):
        par = n % 2
        inc = lambda op: op.then_inc(sem("prep_vec"), 1)
        r, k, v, g = RKVG[n % 3]
        sq, inv = DSM[:, n % 3, 0:8], DSM[:, n % 3, 0:8]
        if part == 1:
            await_step(vec, "prep_pe", "lora", n)
            for i, dst in enumerate((tw, ta)):
                inc(vec.tensor_tensor(dst[:, :, :], PS[6 + i][:, :].rearrange("p (t n) -> p t n", t=2), row(n, W0 + i),
                                      ALU.add))
        if part == 2:
            await_step(vec, "prep_act", "squares", n)
            inc(vec.tensor_reduce(sq, by_head(tq), AX.X, ALU.add))
            await_step(vec, "prep_act", "root", n)
            inc(vec.tensor_scalar(inv, sq, 1e-12, None, ALU.max))
            await_step(vec, "prep_vec", "norm_floor", n)
            inc(vec.reciprocal(inv, inv))
            await_step(vec, "prep_vec", "norm_inverse", n)
            inc(vec.tensor_tensor(by_head(tk), by_head(tk), wide(inv), ALU.mult))
        if part == 3:
            inc(vec.scalar_tensor_tensor(out=tn[:, :, :], in0=ta[:, :, :], scalar=-1.0, in1=row(n, KA), op0=ALU.add,
                                         op1=ALU.mult))
            await_step(vec, "prep_vec", "a1", n)
            inc(vec.scalar_tensor_tensor(out=tn[:, :, :], in0=tn[:, :, :], scalar=1.0, in1=k[:, :, :], op0=ALU.add,
                                         op1=ALU.mult))
            await_step(vec, "prep_act", "growth", n)
            inc(vec.tensor_tensor(tq[:, :, :], PS[6][:, :].rearrange("p (t n) -> p t n", t=2), tw[:, :, :],
                                  ALU.subtract))
            await_step(vec, "prep_pool", "u", n)
            inc(vec.scalar_tensor_tensor(out=NEG_B[par][:, :, :], in0=ta[:, :, :], scalar=-1.0, in1=te[:, :, :],
                                         op0=ALU.mult, op1=ALU.mult))
        if part == 4:
            await_step(vec, "prep_act", "before", n)
            inc(vec.tensor_tensor(tq[:, :, :], tk[:, :, :], tq[:, :, :], ALU.mult))
            await_step(vec, "prep_pool", "rkr", n)
            inc(vec.tensor_reduce(DSM[:, n % 3, 16:24], by_head(tb), AX.X, ALU.add))

    def score_parts():
        return [(t, p, h) for t in range(2) for p in range(2) for h in range(2)]

    def score_pe(pe, n, parts=range(8)):
        par = n % 2
        await_step(pe, "prep_act", "turned3", n)
        for j in parts:
            t, p, h = score_parts()[j]
            if j >= 2:
                await_step(pe, "score_vec", str(j - 2), n)
            f = FR[par][64 * h:64 * h + 64, 2 * t + p, :]
            for kind in range(2):
                mm = pe.matmul(PS[6 + h][:, 256 * kind:256 * kind + 256], f[:, 256 + 128 * kind:384 + 128 * kind],
                               f[:, 0:256], start=True, stop=True)
            mm.then_inc(sem("score_pe"), 1)

    def score_vec(vec, n, parts=range(8)):
        for j in parts:
            t, p, h = score_parts()[j]
            await_step(vec, "score_pe", str(j), n)
            vec.tensor_tensor(MBK[n % 2][:, :, t, 2 * p + h, :], PS[6 + h][:, :].rearrange("p (m s) -> p m s", m=2),
                              both[:, :].unsqueeze(1).to_broadcast([128, 2, 256]), ALU.mult
                              ).then_inc(sem("score_vec"), 1)

    def bcast4(m):
        return m.unsqueeze(1).to_broadcast([128, 4, 128])

    def four(bank):
        return PS[bank][:, :].rearrange("p (h s) -> p h s", h=4)

    def level_pe(pe, n, k, stage):
        inc = lambda op: op.then_inc(sem("level_pe"), 1)
        for t in range(2):
            m, x = MB[n % 2][t], XT[n % 2][t]
            if k == 0:
                await_step(pe, "score_vec", str(4 * t + 3), n)
                for h in range(4):
                    op = pe.transpose(PS[2 * t][:, 128 * h:128 * h + 128], m[:, h, 0:128], ident[:, :])
            elif stage == "Y":
                await_step(pe, "level_vec", f"{k - 1}X{t}", n)
                for h in range(4):
                    op = pe.matmul(PS[2 * t][:, 128 * h:128 * h + 128], m[:, h, 0:128], XI[t][:, h, :],
                                   start=True, stop=True)
            else:
                await_step(pe, "level_vec", f"{k}Y{t}", n)
                if k == 1:
                    await_step(pe, "level_pool", f"T{t}", n)
                else:
                    await_step(pe, "level_vec", f"{k - 1}T{t}", n)
                for h in range(4):
                    if k < 6:
                        pe.matmul(PS[2 * t][:, 128 * h:128 * h + 128], x[:, h, :], YI[t][:, h, :],
                                  start=True, stop=True)
                    op = pe.matmul(PS[2 * t + 1][:, 128 * h:128 * h + 128], YI[t][:, h, :], x[:, h, :],
                                   start=True, stop=True)
            inc(op)

    def level_vec(vec, n, k, stage):
        inc = lambda op: op.then_inc(sem("level_vec"), 1)
        for t in range(2):
            x = XT[n % 2][t]
            if k == 0:
                await_step(vec, "level_pe", f"0Y{t}", n)
                inc(vec.tensor_tensor(YI[t][:, :, :], four(2 * t), bcast4(lev[:, 0, :]), ALU.mult))
                await_step(vec, "level_vec", f"0Y{t}", n)
                inc(vec.tensor_tensor(XI[t][:, :, :], YI[t][:, :, :], bcast4(ident[:, :]), ALU.add))
            elif stage == "Y":
                await_step(vec, "level_pe", f"{k}Y{t}", n)
                inc(vec.tensor_tensor(YI[t][:, :, :], four(2 * t), bcast4(lev[:, k, :]), ALU.mult))
            else:
                await_step(vec, "level_pe", f"{k}Z{t}", n)
                if k < 6:
                    inc(vec.tensor_tensor(XI[t][:, :, :], XI[t][:, :, :], four(2 * t), ALU.add))
                inc(vec.tensor_tensor(x[:, :, :], x[:, :, :], four(2 * t + 1), ALU.add))

    def level_pool(gp, n):
        inc = lambda op: op.then_inc(sem("level_pool"), 1)
        for t in range(2):
            x = XT[n % 2][t]
            await_step(gp, "score_vec", str(4 * t + 3), n)
            inc(gp.tensor_tensor(x[:, :, :], MB[n % 2][t][:, :, 0:128], bcast4(lev0t[:, :]), ALU.mult))
            await_step(gp, "level_pool", f"m{t}", n)
            inc(gp.tensor_tensor(x[:, :, :], x[:, :, :], bcast4(ident[:, :]), ALU.add))

    def state_pe(pe, n, part):
        par = n % 2
        v = RKVG[n % 3][2]
        mb, mk, x = MB[n % 2], MK[n % 2], XT[n % 2]
        inc = lambda op: op.then_inc(sem("state_pe"), 1)

        def right(t):
            for p in range(2):
                c = 256 * t + 128 * p
                if t == 1:
                    pe.matmul(PS[4][:, c:c + 128], FR[par][:, 2 + p, 0:128], U0[:, p, :], start=True, stop=True)
                for h in range(2):
                    op = pe.matmul(PS[4][:, c + 64 * h:c + 64 * h + 64], mk[t][:, 2 * p + h, 0:128],
                                   v[:, t, 128 * p + 64 * h:128 * p + 64 * h + 64], start=(t == 0), stop=True,
                                   skip_group_check=True)
            inc(op)

        def solve(t):
            for h in range(4):
                c = 256 * (1 - t) + 64 * h
                op = pe.matmul(PS[4][:, c:c + 64], x[t][:, h, :], DR[t][:, h, :], start=True, stop=True)
            inc(op)

        def outputs(t):
            for p in range(2):
                c = 256 * t + 128 * p
                if t == 1:
                    pe.matmul(PS[5][:, c:c + 128], FR[par][:, 2 + p, 128:256], U0[:, p, :], start=True, stop=True)
                for h in (2 * p, 2 * p + 1):
                    out = PS[5][:, 256 * t + 64 * h:256 * t + 64 * h + 64]
                    pe.matmul(out, mk[t][:, h, 128:256], v[:, t, 64 * h:64 * h + 64], start=(t == 0), stop=True,
                              skip_group_check=True)
                    op = pe.matmul(out, mb[t][:, h, 128:256], SA[t][:, h, :], start=False, stop=True,
                                   skip_group_check=True)
            inc(op)
        if part == 1:
            await_step(pe, "level_vec", "6T1", n)
            right(0)
        if part == 2:
            await_step(pe, "state_act", "d0", n)
            solve(0)
        if part == 3:
            await_step(pe, "state_act", "s0", n)
            for p in range(2):
                c = slice(128 * p, 128 * p + 128)
                pe.matmul(PS[4][:, c], KH[par][:, 0, c], v[:, 0, c], start=True, stop=False)
                op = pe.matmul(PS[4][:, c], NEG_B[par][:, 0, c], SA[0][:, 2 * p:2 * p + 2, :], start=False, stop=True)
            inc(op)
            if n >= 1:
                await_step(pe, "state_act", "o", n - 1)
            outputs(0)
        if part == 4:
            await_step(pe, "state_vec", "u1", n)
            right(1)
        if part == 5:
            await_step(pe, "state_act", "d1", n)
            solve(1)
        if part == 6:
            await_step(pe, "state_act", "s1", n)
            outputs(1)

    def state_act(act, n, part):
        inc = lambda op: op.then_inc(sem("state_act"), 1)
        if part in (1, 4):
            t = part // 4
            await_step(act, "state_pe", f"d{t}", n)
            inc(act.activation(DR[t][:, :, :], PS[4][:, 256 * t:256 * t + 256].rearrange("p (h e) -> p h e", h=4), ACT.Copy))
        if part in (2, 5):
            t = part // 5
            await_step(act, "state_pe", f"s{t}", n)
            c = 256 * (1 - t)
            inc(act.activation(SA[t][:, :, :], PS[4][:, c:c + 256].rearrange("p (h e) -> p h e", h=4), ACT.Copy))
        if part == 6:
            await_step(act, "state_pe", "o1", n)
            if n >= 1:
                await_step(act, "post_pool", "out", n - 1)
            inc(act.activation(OO[:, :, :], PS[5][:, :].rearrange("p (t n) -> p t n", t=2), ACT.Copy))

    def state_vec(vec, n, part):
        if part != 3:
            return
        await_step(vec, "state_pe", "u", n)
        vec.wait_ge(sem("state_cleared"), 1)
        for h in range(2):
            q = slice(64 * h, 64 * h + 64)
            f = DSM[q, n % 3, 8:10].unsqueeze(2).to_broadcast([64, 2, 64])
            src = PS[4][q, 0:256].rearrange("p (k e) -> p k e", k=2)[:, :, 64 * h:64 * h + 64]
            vec.tensor_tensor(U0[q, :, 64 * h:64 * h + 64], src, f, ALU.mult).then_inc(sem("state_vec"), 1)

    STATE_AT = {h: h for h in range(1, 7)}
    PREP_AT = {2: 1, 4: 2, 5: 3, 6: 4, 7: 5, 8: 6}
    POST_AT = {8: 1, 10: 2, 11: 3, 12: 4}
    SCORE_AT = {9: range(0, 2), 10: range(2, 4), 11: range(4, 6), 12: range(6, 8)}

    def pipeline(eng, level, state, prep, post, score):
        for part in range(1, 7):
            prep(eng, 0, part)
        score(eng, 0, range(8))
        for n in range(GROUPS + 1):
            if n < GROUPS:
                level(eng, n, 0, "Y")
            for half in range(1, 13):
                if n < GROUPS:
                    level(eng, n, (half + 1) // 2, "ZY"[half % 2])
                if n >= 1 and half in STATE_AT:
                    state(eng, n - 1, STATE_AT[half])
                if n + 1 < GROUPS and half in PREP_AT:
                    prep(eng, n + 1, PREP_AT[half])
                if n >= 1 and half in POST_AT:
                    post(eng, n - 1, POST_AT[half])
                if n + 1 < GROUPS and half in SCORE_AT:
                    score(eng, n + 1, SCORE_AT[half])

    def idle(*args):
        pass

    def post_act(act, n, part):
        par = n % 2
        if part == 1:
            act.activation(RKVG[n % 3][3][:, :, :], RKVG[n % 3][3][:, :, :], ACT.Silu).then_inc(sem("post_act"), 1)
        if part == 2:
            await_step(act, "post_vec", "centre", n)
            act.activation(P1[:, :, :], OO[:, :, :], ACT.Square).then_inc(sem("post_act"), 1)
        if part == 3:
            await_step(act, "post_vec", "eps", n)
            act.activation(DSM[:, n % 3, 32:40], DSM[:, n % 3, 32:40], ACT.Sqrt).then_inc(sem("post_act"), 1)

    def post_vec(vec, n, part):
        par = n % 2
        inc = lambda op: op.then_inc(sem("post_vec"), 1)
        m, w = DSM[:, n % 3, 24:32], DSM[:, n % 3, 32:40]
        if part == 1:
            await_step(vec, "state_act", "o", n)
            inc(vec.tensor_reduce(m, by_head(OO), AX.X, ALU.add))
            await_step(vec, "post_vec", "sum", n)
            inc(vec.tensor_scalar(m, m, 1.0 / 64, None, ALU.mult))
            await_step(vec, "post_vec", "mean", n)
            inc(vec.tensor_tensor(by_head(OO), by_head(OO), wide(m), ALU.subtract))
        if part == 2:
            await_step(vec, "post_act", "squares", n)
            inc(vec.tensor_reduce(w, by_head(P1), AX.X, ALU.add))
            await_step(vec, "post_vec", "var", n)
            inc(vec.tensor_scalar(w, w, 1.0 / 64, GN_EPS, ALU.mult, ALU.add))
        if part == 3:
            await_step(vec, "post_act", "root", n)
            inc(vec.reciprocal(w, w))
            await_step(vec, "post_vec", "inverse", n)
            inc(vec.tensor_tensor(by_head(OO), by_head(OO), wide(w), ALU.mult))

    def post_pool(gp, n, part):
        par = n % 2
        inc = lambda op: op.then_inc(sem("post_pool"), 1)
        if part == 1:
            inc(gp.tensor_tensor(by_head(P2), by_head(RKVG[n % 3][2]), wide(DSM[:, n % 3, 16:24]), ALU.mult))
        if part == 4:
            await_step(gp, "post_vec", "norm", n)
            inc(gp.tensor_tensor(OO[:, :, :], OO[:, :, :], row(n, GNW), ALU.mult))
            await_step(gp, "post_pool", "gain", n)
            inc(gp.tensor_tensor(OO[:, :, :], OO[:, :, :], row(n, GNB), ALU.add))
            await_step(gp, "post_pool", "bias", n)
            inc(gp.tensor_tensor(OO[:, :, :], OO[:, :, :], P2[:, :, :], ALU.add))
            await_step(gp, "post_pool", "with_bonus", n)
            await_step(gp, "post_act", "silu", n)
            inc(gp.tensor_tensor(OT[:, :, GW * n:GW * n + GW], OO[:, :, :], RKVG[n % 3][3][:, :, :], ALU.mult))

    def d_ready(e):
        if "C" in segments:
            e.wait_ge(sem("even_normed"), 2)
        else:
            e.wait_ge(sem("x_loaded"), 16)

    MU = {"r": 0, "w": 1, "k": 2, "v": 3, "a": 4, "g": 5}
    ORDER = "rwakvg"
    GEMMS = "rkvg"

    def d_pool(gp):
        d_ready(gp)
        gp.dma_start(XKEPT2, X[:, :, :]).then_inc(sem("x_kept2"), 16)
        for i, name in enumerate(("od_w1_2", "od_a1_2")):
            gp.dma_start(LW[i][:, :, :], a[name][0].rearrange("(k p) n -> p k n", p=128)).then_inc(sem("lora_loaded"), 16)
        n = 0
        for k, name in enumerate(GEMMS):
            j = plan["odd_" + name]
            for p in range(4):
                gp.wait_ge(sem("acc_free"), j.p0 + p + 3)
                gp.dma_start(kept[k].rearrange("(t p) d -> p t d", p=128)[:, :, PANEL * p:PANEL * p + PANEL],
                             DS[p % 2][:, :, :]).then_inc(sem(f"rkvg_stored{p % 2}"), 16)
        for par in range(2):
            gp.wait_ge(sem(f"rkvg_stored{par}"), 16 * 8)
        gp.memset(U0[:, :, :], 0.0).then_inc(sem("state_cleared"), 1)
        first = tables["level0"][0]
        gp.dma_start(d_tables[:, :], a["tables"][:, first:first + D_TABLES]).then_inc(sem("d_loaded"), 16)
        gp.wait_ge(sem("d_loaded"), 16)
        pipeline(gp, lambda e, n, k, stage: level_pool(e, n) if k == 0 else None, idle, prep_pool, post_pool, idle)
        gp.wait_ge(sem("turned"), TD_o.first + 8)
        gp.wait_ge(sem("x_kept2"), 16)
        gp.dma_start(X[:, :, :], XKEPT2).then_inc(sem("x_back2"), 16)
        for i, nm in enumerate(("ln_g_2", "ln_b_2")):
            gp.dma_start(LD[:, i, :], a[nm][1].partition_broadcast(128)).then_inc(sem("d_norm_loaded"), 16)

    def d_pe(pe):
        turn_pe(pe, TD_x, lambda k, t: X[:, t, 128 * k:128 * k + 128], lambda n: d_ready(pe))

        def lora(i):
            pe.wait_ge(sem("lora_loaded"), 32)
            pe.wait_ge(sem("mixed"), 4 * (2 + i))
            for k in range(KT):
                mm = pe.matmul(PS[4 + i][0:LORA, 0:S], LW[i][:, k, :], MT[:, k, :], start=(k == 0), stop=(k == KT - 1))
            mm.then_inc(sem("lora_products"), 1)
        for n, name in enumerate(GEMMS):
            run_pe(pe, plan["odd_" + name], (lambda n: lambda c, k: pe.wait_ge(sem("mix_low_made"), 4 * n + c + 1)
                                             if k == 0 else None)(n),
                   (lambda p: lora(p) if p < 2 else None) if n == 0 else None)
        pe.wait_ge(sem("d_loaded"), 16)
        pipeline(pe, level_pe, state_pe, prep_pe, idle, score_pe)
        await_step(pe, "state_act", "o", GROUPS - 1)
        turn_pe(pe, TD_o, lambda k, t: OT[:, t, 128 * k:128 * k + 128],
                lambda n: await_step(pe, "post_pool", "out", n))
        run_pe(pe, plan["odd_out"], turned_ready(pe, TD_o))

    def d_act(act):
        def high(n, i):
            k = slice(4 * i, 4 * i + 4)
            act.wait_ge(sem("mixed"), 4 * (0, 3, 4, 5)[n] + i + 1)
            act.activation(dh[n % 2][:, k, :], MT[:, k, :], ACT.Copy).then_inc(sem("mix_high_made"), 1)
        for n in range(8):
            m = TD_x.first + n
            act.wait_ge(sem("turned"), m + 1)
            act.activation(xT[:, 2 * n:2 * n + 2, :], PS[4 + m % 4][:, :].rearrange("p (k s) -> p k s", k=2), ACT.Copy
                           ).then_inc(sem("turned_read"), 1)
            if n % 2 == 1 and n >= 3:
                high(0, n // 2 - 1)
        high(0, 3)
        stores = [0]

        def free(p):
            if stores[0] >= 2:
                act.wait_ge(sem(f"rkvg_stored{p % 2}"), 16 * (stores[0] // 2))
            stores[0] += 1

        def lora(i):
            act.wait_ge(sem("lora_products"), i + 1)
            act.activation(TH[:, i, :], PS[4 + i][0:LORA, 0:S], ACT.Tanh if i == 0 else ACT.Copy
                           ).then_inc(sem("lora_hidden"), 1)
        for n, name in enumerate(GEMMS):
            def post(p, n=n):
                if n == 0 and p in (1, 2):
                    lora(p - 1)

            def each(c, n=n):
                first = 12 if n == 0 else 5
                if n < 3 and first <= c < first + 4:
                    high(n + 1, c - first)
            run_act(act, plan["odd_" + name], lambda p, t: DS[p % 2][:, t, :], free, post, each)
        pipeline(act, idle, state_act, prep_act, post_act, idle)
        turn_high(act, TD_o, oh)
        run_act(act, plan["odd_out"], lambda p, t: YD[:, t, PANEL * p:PANEL * p + PANEL])
        norm_act(act, 1)

    def d_vec(vec):
        def shift(i):
            k = slice(4 * i, 4 * i + 4)
            vec.wait_ge(sem("turned_read"), TD_x.first + 2 * i + 2)
            vec.tensor_tensor(xx[:, k, 1:S], xT[:, k, 0:S - 1], xT[:, k, 1:S], ALU.subtract)
            vec.tensor_scalar(xx[:, k, 0:1], xT[:, k, 0:1], -1.0, None, ALU.mult).then_inc(sem("shift_made"), 1)

        def mixed(name, i):
            if name in "ak":
                vec.wait_ge(sem("lora_products"), "ak".index(name) + 1)
            for k in range(4 * i, 4 * i + 4):
                c = 32 + 16 * MU[name] + k
                op = vec.scalar_tensor_tensor(out=MT[:, k, :], in0=xx[:, k, :], scalar=gains[:, c:c + 1],
                                              in1=xT[:, k, :], op0=ALU.mult, op1=ALU.add)
            op.then_inc(sem("mixed"), 1)

        def low(n, i):
            k = slice(4 * i, 4 * i + 4)
            vec.wait_ge(sem("mix_high_made"), 4 * n + i + 1)
            vec.tensor_tensor(dl[n % 2][:, k, :], MT[:, k, :], dh[n % 2][:, k, :].bitcast(F32), ALU.subtract
                              ).then_inc(sem("mix_low_made"), 1)
        shift(0)
        for i in range(4):
            if i < 3:
                shift(i + 1)
            vec.wait_ge(sem("shift_made"), i + 1)
            mixed("r", i)
            if i:
                low(0, i - 1)
        low(0, 3)
        for n, name in enumerate(GEMMS):
            def each(c, n=n):
                if n == 0:
                    if c < 12:
                        mixed("wak"[c // 4], c % 4)
                    else:
                        low(1, c - 12)
                elif n < 3 and c < 4:
                    mixed(GEMMS[n + 1], c)
                elif n < 3 and 5 <= c < 9:
                    low(n + 1, c - 5)
            run_vec(vec, plan["odd_" + name], None, each)
        pipeline(vec, level_vec, state_vec, prep_vec, post_vec, score_vec)
        turn_low(vec, TD_o, oh, ol)
        run_vec(vec, plan["odd_out"])
        vec.wait_ge(sem("x_back2"), 16)
        norm_vec(vec, YD, LD, "d_norm_loaded", plan["odd_out"], "odd_normed", 1)

    segs["D"] = (d_pe, d_act, d_vec, d_pool)
    with nc.Block() as block:
        @block.sync
        def _(sp):
            load_weights(sp)
            name, n = last[segments[-1]]
            sp.wait_ge(sem(name), n)
            sp.dma_start(OUTR, X[:, :, :]).then_inc(sem("stored"), 16)
            sp.wait_ge(sem("stored"), 16)

        @block.tensor
        def _(pe):
            start_pe(pe)
            for s in segments:
                segs[s][0](pe)

        @block.scalar
        def _(act):
            start_act(act)
            splits_begin(act, True)
            for s in segments:
                segs[s][1](act)

        @block.vector
        def _(vec):
            start_vec(vec)
            splits_begin(vec, False)
            for s in segments:
                segs[s][2](vec)

        @block.gpsimd
        def _(gp):
            for s in segments:
                segs[s][3](gp)
    ctx.close()


INPUTS = ["x", "rel_bias_table", "w_in", "b_gate", "lam_q1", "lam_k1", "lam_q2", "lam_k2", "diff_subln_g",
          "sinks", "w_oa", "w_ob", "w_oc", "w_out", "pre_mix_g", "post_mix_g", "pre_ffn_g", "post_ffn_g",
          "w_up", "conv_w", "conv_b", "w_down", "ev_w_in_2", "ev_w_pool_2", "ev_pool_scale_2", "ev_w_out_2",
          "od_mu_2", "od_w_r_2", "od_w_k_2", "od_w_v_2", "od_w_g_2", "od_w0_2", "od_w1_2", "od_w2_2",
          "od_a0_2", "od_a1_2", "od_a2_2", "od_k_k_2", "od_k_a_2", "od_r_k_2", "od_gn_w_2", "od_gn_b_2",
          "od_w_o_2", "ln_g_2", "ln_b_2"]


def kernel(**inputs):
    import concourse.bacc as bacc
    from concourse.bass_utils import run_bass_kernel_spmd

    nc = bacc.Bacc("TRN2", target_bir_lowering=False, num_devices=1)
    arrays, args = {}, {}
    for name in INPUTS:
        v = np.ascontiguousarray(inputs[name])
        arrays[f"in_{name}"] = v
        args[name] = nc.dram_tensor(f"in_{name}", v.shape, mybir.dt.from_np(v.dtype), kind="ExternalInput").ap()
    tables = np.ascontiguousarray(np.concatenate(list(constant_tables().values()), axis=1))
    arrays["in_tables"] = tables
    args["tables"] = nc.dram_tensor("in_tables", tables.shape, F32, kind="ExternalInput").ap()
    args["out"] = nc.dram_tensor("out_0", (1, S, D), F32, kind="ExternalOutput").ap()
    build(nc, args)
    result = run_bass_kernel_spmd(nc, [arrays], core_ids=[0])
    return result.results[0]["out_0"]
```
